# Optimizing a Trainium2 kernel written in Bass

```python
import math
import jax
import jax.numpy as jnp
from jax import lax
import numpy as np

D_MODEL = 1024
BATCH = 1
SEQ = 1024
DEPTH = 2

CTX_LEN = 256
GRID_W = 64
HEAD_DIM = 64
MIX_W = D_MODEL
A_HEADS = D_MODEL // (4 * HEAD_DIM)
A_DK = HEAD_DIM // 2
A_DV = HEAD_DIM
A_W = A_HEADS * HEAD_DIM
B_HEADS = 3 * D_MODEL // (8 * HEAD_DIM)
B_KV_HEADS = 2
B_W = B_HEADS * HEAD_DIM
B_KV_W = B_KV_HEADS * HEAD_DIM
C_HEADS = 3 * D_MODEL // (8 * HEAD_DIM)
C_W = C_HEADS * HEAD_DIM
WIN_H = 8
WIN_W = 16
Q_BLOCK = 128
ROPE_THETA = 10000.0
EPS = 1e-6
SPLIT_SIZES = (A_W, A_W, A_W, A_W, B_W, B_KV_W, B_KV_W, B_W, C_W, C_W, C_W, C_W)
IN_W = sum(SPLIT_SIZES)


def rms_norm(x, g):
    xf = x.astype(jnp.float32)
    y = xf * lax.rsqrt(jnp.mean(xf * xf, axis=-1, keepdims=True) + EPS)
    return (y * g.astype(jnp.float32)).astype(x.dtype)

def axial_rope(x, row, col):
    d = x.shape[-1]
    nf = d // 4
    inv = ROPE_THETA ** (-jnp.arange(nf, dtype=jnp.float32) / nf)
    ang = jnp.concatenate([row[:, None] * inv, col[:, None] * inv], axis=-1)
    shape = (1, x.shape[1]) + (1,) * (x.ndim - 3) + (d // 2,)
    cos = jnp.cos(ang).reshape(shape)
    sin = jnp.sin(ang).reshape(shape)
    xf = x.astype(jnp.float32)
    x1, x2 = xf[..., : d // 2], xf[..., d // 2:]
    return jnp.concatenate([x1 * cos - x2 * sin, x2 * cos + x1 * sin], axis=-1).astype(x.dtype)

def map_query_blocks(fn, q):
    b, s = q.shape[:2]
    nb = s // Q_BLOCK
    qb = jnp.moveaxis(q.reshape((b, nb, Q_BLOCK) + q.shape[2:]), 1, 0)
    out = lax.map(fn, qb)
    return jnp.moveaxis(out, 0, 1).reshape((b, s) + out.shape[3:])

def diff_attend(q, k, v, lam):
    s = jnp.einsum('bqhmd,bkhmd->bhmqk', q, k).astype(jnp.float32) * (q.shape[-1] ** -0.5)
    p = jax.nn.softmax(s, axis=-1)
    a = (p[:, :, 0] - lam * p[:, :, 1]).astype(v.dtype)
    return jnp.einsum('bhqk,bkhd->bqhd', a, v)

def gqa_attend(q, k, v):
    b, nq, h, d = q.shape
    kvh = k.shape[2]
    qg = q.reshape(b, nq, kvh, h // kvh, d)
    s = jnp.einsum('bqhgd,bkhd->bhgqk', qg, k).astype(jnp.float32) * (d ** -0.5)
    p = jax.nn.softmax(s, axis=-1).astype(v.dtype)
    o = jnp.einsum('bhgqk,bkhd->bqhgd', p, v)
    return o.reshape(b, nq, h * v.shape[-1])

def neighbourhood_attend(q, k, v, k_ctx, v_ctx, rpb, rows):
    b, s, h, d = q.shape
    kh = min(WIN_H, rows)
    kw = WIN_W
    scale = d ** -0.5
    qg = q.reshape(b, rows, GRID_W, h, d)
    kg = k.reshape(b, rows, GRID_W, h, d)
    vg = v.reshape(b, rows, GRID_W, h, d)
    r = jnp.arange(rows)
    cidx = jnp.arange(GRID_W)
    r0 = jnp.clip(r - kh // 2, 0, rows - kh)
    key_rows = r0[:, None] + jnp.arange(kh)
    k_blk = kg[:, key_rows]
    v_blk = vg[:, key_rows]
    c0 = jnp.clip(cidx - kw // 2, 0, GRID_W - kw)
    in_win = (cidx[None, :] >= c0[:, None]) & (cidx[None, :] < c0[:, None] + kw)
    dr = key_rows - r[:, None] + (WIN_H - 1)
    dc = jnp.clip(cidx[None, :] - cidx[:, None] + (WIN_W - 1), 0, 2 * WIN_W - 2)
    bias = rpb[:, dr[:, None, :, None], dc[None, :, None, :]]
    s_nb = jnp.einsum('brqhd,brkwhd->bhrqkw', qg, k_blk).astype(jnp.float32) * scale
    s_nb = s_nb + bias.astype(jnp.float32)[None]
    s_nb = jnp.where(in_win[:, None, :], s_nb, -jnp.inf)
    s_cx = jnp.einsum('brqhd,bchd->bhrqc', qg, k_ctx).astype(jnp.float32) * scale
    n_nb = kh * GRID_W
    sc = jnp.concatenate([s_nb.reshape(b, h, rows, GRID_W, n_nb), s_cx], axis=-1)
    p = jax.nn.softmax(sc, axis=-1).astype(v.dtype)
    p_nb = p[..., :n_nb].reshape(b, h, rows, GRID_W, kh, GRID_W)
    p_cx = p[..., n_nb:]
    o = jnp.einsum('bhrqkw,brkwhd->brqhd', p_nb, v_blk) + jnp.einsum('bhrqc,bchd->brqhd', p_cx, v_ctx)
    return o.reshape(b, s, h * d)

def split_proj(p):
    idx = np.cumsum(SPLIT_SIZES)[:-1].tolist()
    return jnp.split(p, idx, axis=-1)

def first_inputs(seed: int = 0) -> dict:
    key = jax.random.key(seed)
    ks = jax.random.split(key, 22)
    nrm = jax.random.normal
    f32 = jnp.float32
    return {
        'x': nrm(ks[0], (BATCH, SEQ, D_MODEL), f32),
        'c': nrm(ks[1], (BATCH, D_MODEL), f32),
        'ctx': nrm(ks[2], (BATCH, CTX_LEN, D_MODEL), f32),
        'c_ctx': nrm(ks[3], (D_MODEL,), f32),
        'norm_g': 1.0 + 0.05 * nrm(ks[4], (DEPTH, D_MODEL), f32),
        'w_ada': nrm(ks[5], (DEPTH, D_MODEL, 3 * D_MODEL), f32) * (0.5 * D_MODEL ** -0.5),
        'b_ada': 0.01 * nrm(ks[6], (DEPTH, 3 * D_MODEL), f32),
        'w_in': nrm(ks[7], (DEPTH, D_MODEL, IN_W), f32) * (D_MODEL ** -0.5),
        'w_out': nrm(ks[8], (DEPTH, MIX_W, D_MODEL), f32) * (MIX_W ** -0.5),
        'diff_q_norm': 1.0 + 0.05 * nrm(ks[9], (DEPTH, A_DK), f32),
        'diff_k_norm': 1.0 + 0.05 * nrm(ks[10], (DEPTH, A_DK), f32),
        'lambda_q1': 0.1 * nrm(ks[11], (DEPTH, A_DK), f32),
        'lambda_k1': 0.1 * nrm(ks[12], (DEPTH, A_DK), f32),
        'lambda_q2': 0.1 * nrm(ks[13], (DEPTH, A_DK), f32),
        'lambda_k2': 0.1 * nrm(ks[14], (DEPTH, A_DK), f32),
        'diff_subln': 1.0 + 0.05 * nrm(ks[15], (DEPTH, A_DV), f32),
        'gqa_q_norm': 1.0 + 0.05 * nrm(ks[16], (DEPTH, HEAD_DIM), f32),
        'gqa_k_norm': 1.0 + 0.05 * nrm(ks[17], (DEPTH, HEAD_DIM), f32),
        'nat_q_norm': 1.0 + 0.05 * nrm(ks[18], (DEPTH, HEAD_DIM), f32),
        'nat_k_norm': 1.0 + 0.05 * nrm(ks[19], (DEPTH, HEAD_DIM), f32),
        'nat_rpb': 0.1 * nrm(ks[20], (DEPTH, C_HEADS, 2 * WIN_H - 1, 2 * WIN_W - 1), f32),
    }

def first_block(x, c, ctx, c_ctx, norm_g, w_ada, b_ada, w_in, w_out, diff_q_norm, diff_k_norm,
              lambda_q1, lambda_k1, lambda_q2, lambda_k2, diff_subln, gqa_q_norm, gqa_k_norm,
              nat_q_norm, nat_k_norm, nat_rpb):
    b, s, _ = x.shape
    n_ctx = ctx.shape[1]
    rows = s // GRID_W
    t = jnp.arange(s)
    row = (t // GRID_W).astype(jnp.float32)
    col = (t % GRID_W).astype(jnp.float32)
    for l in range(DEPTH):
        lam_init = 0.8 - 0.6 * math.exp(-0.3 * l)
        sh, sc, gt = jnp.split(jax.nn.silu(c) @ w_ada[l] + b_ada[l], 3, axis=-1)
        sh_c, sc_c, gt_c = jnp.split(jax.nn.silu(c_ctx) @ w_ada[l] + b_ada[l], 3, axis=-1)
        h = rms_norm(x, norm_g[l]) * (1 + sc[:, None]) + sh[:, None]
        hc = rms_norm(ctx, norm_g[l]) * (1 + sc_c) + sh_c
        qa, ka, va, ga, qb, kb, vb, gb, qn, kn, vn, gn = split_proj(h @ w_in[l])
        qa_c, ka_c, va_c, ga_c, qb_c, kb_c, vb_c, gb_c, qn_c, kn_c, vn_c, gn_c = split_proj(hc @ w_in[l])

        lam = (jnp.exp(jnp.sum(lambda_q1[l] * lambda_k1[l])) - jnp.exp(jnp.sum(lambda_q2[l] * lambda_k2[l]))
               + lam_init).astype(jnp.float32)
        qa = axial_rope(rms_norm(qa.reshape(b, s, A_HEADS, 2, A_DK), diff_q_norm[l]), row, col)
        ka = axial_rope(rms_norm(ka.reshape(b, s, A_HEADS, 2, A_DK), diff_k_norm[l]), row, col)
        ka_c = rms_norm(ka_c.reshape(b, n_ctx, A_HEADS, 2, A_DK), diff_k_norm[l])
        va_c = va_c.reshape(b, n_ctx, A_HEADS, A_DV)
        ka_all = jnp.concatenate([ka, ka_c], axis=1)
        va_all = jnp.concatenate([va.reshape(b, s, A_HEADS, A_DV), va_c], axis=1)
        oa = map_query_blocks(lambda q_blk: diff_attend(q_blk, ka_all, va_all, lam), qa)
        ya = (rms_norm(oa, diff_subln[l]) * (1 - lam_init)).reshape(b, s, A_W) * jax.nn.silu(ga)

        qb = axial_rope(rms_norm(qb.reshape(b, s, B_HEADS, HEAD_DIM), gqa_q_norm[l]), row, col)
        kb = axial_rope(rms_norm(kb.reshape(b, s, B_KV_HEADS, HEAD_DIM), gqa_k_norm[l]), row, col)
        kb_c = rms_norm(kb_c.reshape(b, n_ctx, B_KV_HEADS, HEAD_DIM), gqa_k_norm[l])
        vb_c = vb_c.reshape(b, n_ctx, B_KV_HEADS, HEAD_DIM)
        kb_all = jnp.concatenate([kb, kb_c], axis=1)
        vb_all = jnp.concatenate([vb.reshape(b, s, B_KV_HEADS, HEAD_DIM), vb_c], axis=1)
        yb = map_query_blocks(lambda q_blk: gqa_attend(q_blk, kb_all, vb_all), qb) * jax.nn.silu(gb)

        qn = rms_norm(qn.reshape(b, s, C_HEADS, HEAD_DIM), nat_q_norm[l])
        kn = rms_norm(kn.reshape(b, s, C_HEADS, HEAD_DIM), nat_k_norm[l])
        kn_c = rms_norm(kn_c.reshape(b, n_ctx, C_HEADS, HEAD_DIM), nat_k_norm[l])
        vn_c = vn_c.reshape(b, n_ctx, C_HEADS, HEAD_DIM)
        yn = neighbourhood_attend(qn, kn, vn.reshape(b, s, C_HEADS, HEAD_DIM), kn_c, vn_c, nat_rpb[l], rows)
        yn = yn * jax.nn.silu(gn)

        y = jnp.concatenate([ya, yb, yn], axis=-1) @ w_out[l]

        if l < DEPTH - 1:
            qa_c = rms_norm(qa_c.reshape(b, n_ctx, A_HEADS, 2, A_DK), diff_q_norm[l])
            oa_c = diff_attend(qa_c, ka_c, va_c, lam)
            ya_c = (rms_norm(oa_c, diff_subln[l]) * (1 - lam_init)).reshape(b, n_ctx, A_W) * jax.nn.silu(ga_c)
            qb_c = rms_norm(qb_c.reshape(b, n_ctx, B_HEADS, HEAD_DIM), gqa_q_norm[l])
            yb_c = gqa_attend(qb_c, kb_c, vb_c) * jax.nn.silu(gb_c)
            qn_c = rms_norm(qn_c.reshape(b, n_ctx, C_HEADS, HEAD_DIM), nat_q_norm[l])
            yn_c = gqa_attend(qn_c, kn_c, vn_c) * jax.nn.silu(gn_c)
            ctx = ctx + gt_c * (jnp.concatenate([ya_c, yb_c, yn_c], axis=-1) @ w_out[l])

        x = x + gt[:, None] * y
    return x


DEPTH_2 = 1

N_META = 16
CHUNK = 128
PAD = CHUNK - N_META
SB_HEADS = 4
SB_W = SB_HEADS * HEAD_DIM
SSD_HEADS = 8
SSD_W = SSD_HEADS * HEAD_DIM
SSD_GROUPS = 2
SSD_STATE = 128
SSD_CONV = 4
SSD_CONV_DIM = SSD_W + 2 * SSD_GROUPS * SSD_STATE
HG_HEADS = 4
HG_DK = 64
HG_DV = 64
HG_W = HG_HEADS * HG_DV
D_MIX = SB_W + SSD_W + HG_W
D_FF = 4 * D_MODEL
TINY = 1e-30
IN_SIZES = (SB_W, SB_W, SB_W,
            SSD_W, SSD_W, SSD_GROUPS * SSD_STATE, SSD_GROUPS * SSD_STATE, SSD_HEADS,
            HG_HEADS * HG_DK, HG_HEADS * HG_DK, HG_W, HG_W)
D_IN = 3 * SB_W + 2 * SSD_W + 2 * SSD_GROUPS * SSD_STATE + SSD_HEADS + 2 * HG_HEADS * HG_DK + 2 * HG_W


def rmsnorm(x, w):
    xf = x.astype(jnp.float32)
    y = xf * lax.rsqrt(jnp.mean(xf * xf, axis=-1, keepdims=True) + EPS)
    return (y * w.astype(jnp.float32)).astype(x.dtype)

def causal_depthwise_conv(u, w, b):
    y = lax.conv_general_dilated(
        u, w[:, None, :].astype(u.dtype), window_strides=(1,), padding=[(w.shape[0] - 1, 0)],
        dimension_numbers=('NWC', 'WIO', 'NWC'), feature_group_count=u.shape[-1])
    return y + b.astype(u.dtype)

def to_chunks(t):
    b, l = t.shape[:2]
    return jnp.moveaxis(t.reshape((b, l // CHUNK, CHUNK) + t.shape[2:]), 1, 0)

def from_chunks(t):
    n, b = t.shape[:2]
    return jnp.moveaxis(t, 0, 1).reshape((b, n * CHUNK) + t.shape[3:])

def masked_decay(seg, mask):
    return jnp.where(mask, jnp.exp(jnp.where(mask, seg, 0.0)), 0.0)

def stick_breaking_attention(q, k, v, valid):
    L, dh = q.shape[2], q.shape[3]
    scale = dh ** -0.5
    pos = jnp.arange(L)
    outs = []
    for blk in range(L // CHUNK):
        start, end = blk * CHUNK, (blk + 1) * CHUNK
        z = jnp.einsum('bhqd,bhkd->bhqk', q[:, :, start:end], k[:, :, :end]).astype(jnp.float32) * scale
        mask = (pos[None, :end] < pos[start:end, None]) & valid[None, :end]
        log_keep = jnp.where(mask, jax.nn.log_sigmoid(-z), 0.0)
        csum = jnp.cumsum(log_keep, axis=-1)
        log_w = jax.nn.log_sigmoid(z) + (csum[..., -1:] - csum)
        w = jnp.where(mask, jnp.exp(jnp.where(mask, log_w, 0.0)), 0.0)
        outs.append(jnp.einsum('bhqk,bhkd->bhqd', w.astype(v.dtype), v[:, :, :end]))
    return jnp.concatenate(outs, axis=2)

def stick_breaking_group(q, k, v, q_norm, k_norm, out_norm, valid):
    bsz, L, _ = q.shape
    shp = (bsz, L, SB_HEADS, HEAD_DIM)
    qh = jnp.transpose(rmsnorm(q.reshape(shp), q_norm), (0, 2, 1, 3))
    kh = jnp.transpose(rmsnorm(k.reshape(shp), k_norm), (0, 2, 1, 3))
    vh = jnp.transpose(v.reshape(shp), (0, 2, 1, 3))
    o = jnp.transpose(stick_breaking_attention(qh, kh, vh, valid), (0, 2, 1, 3))
    return rmsnorm(o, out_norm).reshape(bsz, L, SB_W)

def ssd_chunked(xdt, a, bm, cm):
    bsz = xdt.shape[0]
    rep = SSD_HEADS // SSD_GROUPS
    causal = jnp.tril(jnp.ones((CHUNK, CHUNK), dtype=bool))

    def step(state, inp):
        a_c, x_c, b_c, c_c = inp
        acum = jnp.cumsum(a_c, axis=1)
        seg = acum[:, :, None, :] - acum[:, None, :, :]
        decay = masked_decay(seg, causal[None, :, :, None])
        cb = jnp.repeat(jnp.einsum('btgn,bsgn->btsg', c_c, b_c), rep, axis=-1)
        y_diag = jnp.einsum('btsh,bshp->bthp', cb * decay, x_c)
        c_h = jnp.repeat(c_c, rep, axis=2)
        b_h = jnp.repeat(b_c, rep, axis=2)
        y_off = jnp.einsum('bthn,bhpn->bthp', c_h, state) * jnp.exp(acum)[..., None]
        w_end = jnp.exp(acum[:, -1:, :] - acum)
        state = state * jnp.exp(acum[:, -1, :])[:, :, None, None] + jnp.einsum('bshn,bsh,bshp->bhpn', b_h, w_end, x_c)
        return state, y_diag + y_off

    state0 = jnp.zeros((bsz, SSD_HEADS, HEAD_DIM, SSD_STATE), jnp.float32)
    xs = tuple(to_chunks(t.astype(jnp.float32)) for t in (a, xdt, bm, cm))
    _, y = lax.scan(step, state0, xs)
    return from_chunks(y)

def ssd_group(z, xs, bm, cm, dt_raw, conv_w, conv_b, dt_bias, a_log, d_skip, norm_w, vmask):
    bsz, L, _ = xs.shape
    f32 = jnp.float32
    xbc = jax.nn.silu(causal_depthwise_conv(jnp.concatenate([xs, bm, cm], axis=-1) * vmask, conv_w, conv_b))
    xs, bm, cm = jnp.split(xbc, [SSD_W, SSD_W + SSD_GROUPS * SSD_STATE], axis=-1)
    dt = jax.nn.softplus(dt_raw.astype(f32) + dt_bias.astype(f32)) * vmask.astype(f32)
    a_neg = -jnp.exp(a_log.astype(f32))
    xh = xs.reshape(bsz, L, SSD_HEADS, HEAD_DIM).astype(f32)
    y = ssd_chunked(xh * dt[..., None], dt * a_neg,
                    bm.reshape(bsz, L, SSD_GROUPS, SSD_STATE), cm.reshape(bsz, L, SSD_GROUPS, SSD_STATE))
    y = y + xh * d_skip.astype(f32)[:, None]
    y = y.reshape(bsz, L, SSD_W) * jax.nn.silu(z.astype(f32))
    y = rmsnorm(y.reshape(bsz, L, SSD_GROUPS, SSD_W // SSD_GROUPS), norm_w)
    return y.reshape(bsz, L, SSD_W).astype(z.dtype)

def hgrn2_chunked(q, k, v, log_f):
    bsz = q.shape[0]
    causal = jnp.tril(jnp.ones((CHUNK, CHUNK), dtype=bool))

    def step(S, inp):
        q_c, k_c, v_c, g_c = inp
        gcum = jnp.cumsum(g_c, axis=1)
        seg = gcum[:, :, None] - gcum[:, None, :]
        decay = masked_decay(seg, causal[None, :, :, None, None])
        scores = jnp.einsum('bthk,btshk,bshk->btsh', q_c, decay, k_c)
        o_intra = jnp.einsum('btsh,bshv->bthv', scores, v_c)
        o_inter = jnp.einsum('bthk,bhkv->bthv', q_c * jnp.exp(gcum), S)
        k_end = k_c * jnp.exp(gcum[:, -1:] - gcum)
        S = S * jnp.exp(gcum[:, -1])[..., None] + jnp.einsum('bshk,bshv->bhkv', k_end, v_c)
        return S, o_intra + o_inter

    S0 = jnp.zeros((bsz, HG_HEADS, HG_DK, HG_DV), jnp.float32)
    _, o = lax.scan(step, S0, tuple(to_chunks(t) for t in (q, k, v, log_f)))
    return from_chunks(o)

def hgrn2_group(q, f_logit, i_in, g, lb, out_norm, valid):
    bsz, L, _ = q.shape
    f32 = jnp.float32
    fl = f_logit.astype(f32)
    keep = valid[None, :, None]
    f = lb + (1.0 - lb) * jax.nn.sigmoid(fl)
    log_f = jnp.where(keep, jnp.log(jnp.maximum(f, TINY)), 0.0)
    k = jnp.where(keep, (1.0 - lb) * jax.nn.sigmoid(-fl), 0.0)
    v = jnp.where(keep, i_in.astype(f32), 0.0)
    qf = jax.nn.silu(q.astype(f32))
    shp = (bsz, L, HG_HEADS, HG_DK)
    o = hgrn2_chunked(qf.reshape(shp), k.reshape(shp), v.reshape(bsz, L, HG_HEADS, HG_DV), log_f.reshape(shp))
    o = rmsnorm(o, out_norm) * jax.nn.silu(g.astype(f32)).reshape(bsz, L, HG_HEADS, HG_DV)
    return o.reshape(bsz, L, HG_W).astype(q.dtype)

def second_inputs(seed: int = 0) -> dict:
    key = jax.random.key(seed)
    ks = jax.random.split(key, 19)
    f32 = jnp.float32

    def normal(k, shape, scale):
        return scale * jax.random.normal(k, shape, f32)

    def gain(k, shape):
        return 1.0 + 0.01 * jax.random.normal(k, shape, f32)

    dt_init = jnp.exp(jax.random.uniform(ks[10], (DEPTH_2, SSD_HEADS), f32,
                                         minval=math.log(1e-3), maxval=math.log(1e-1)))
    return {
        'x': normal(ks[0], (BATCH, SEQ, D_MODEL), 1.0),
        'meta_tokens': normal(ks[1], (N_META, D_MODEL), 1.0),
        'hg_lb_logits': normal(ks[2], (DEPTH_2, HG_HEADS * HG_DK), 0.5),
        'norm_mix_w': gain(ks[3], (DEPTH_2, D_MODEL)),
        'w_in': normal(ks[4], (DEPTH_2, D_MODEL, D_IN), D_MODEL ** -0.5),
        'sb_q_norm': gain(ks[5], (DEPTH_2, HEAD_DIM)),
        'sb_k_norm': gain(ks[6], (DEPTH_2, HEAD_DIM)),
        'sb_out_norm': gain(ks[7], (DEPTH_2, SB_HEADS, HEAD_DIM)),
        'ssd_conv_w': normal(ks[8], (DEPTH_2, SSD_CONV, SSD_CONV_DIM), SSD_CONV ** -0.5),
        'ssd_conv_b': normal(ks[9], (DEPTH_2, SSD_CONV_DIM), 0.01),
        'ssd_dt_bias': dt_init + jnp.log(-jnp.expm1(-dt_init)),
        'ssd_A_log': jnp.log(jax.random.uniform(ks[11], (DEPTH_2, SSD_HEADS), f32, minval=1.0, maxval=16.0)),
        'ssd_D': gain(ks[12], (DEPTH_2, SSD_HEADS)),
        'ssd_norm_w': gain(ks[13], (DEPTH_2, SSD_GROUPS, SSD_W // SSD_GROUPS)),
        'hg_out_norm': gain(ks[14], (DEPTH_2, HG_HEADS, HG_DV)),
        'w_out': normal(ks[15], (DEPTH_2, D_MIX, D_MODEL), D_MIX ** -0.5),
        'norm_mlp_w': gain(ks[16], (DEPTH_2, D_MODEL)),
        'w_up': normal(ks[17], (DEPTH_2, D_MODEL, D_FF), D_MODEL ** -0.5),
        'w_down': normal(ks[18], (DEPTH_2, D_FF, D_MODEL), D_FF ** -0.5),
    }

def second_block(x, meta_tokens, hg_lb_logits, norm_mix_w, w_in, sb_q_norm, sb_k_norm, sb_out_norm,
              ssd_conv_w, ssd_conv_b, ssd_dt_bias, ssd_A_log, ssd_D, ssd_norm_w, hg_out_norm,
              w_out, norm_mlp_w, w_up, w_down):
    bsz = x.shape[0]
    dtype = x.dtype
    lead = jnp.concatenate([jnp.zeros((PAD, D_MODEL), dtype), meta_tokens.astype(dtype)], axis=0)
    h = jnp.concatenate([jnp.broadcast_to(lead[None], (bsz, CHUNK, D_MODEL)), x], axis=1)
    L = h.shape[1]
    valid = jnp.arange(L) >= PAD
    vmask = valid[None, :, None].astype(dtype)
    probs = jax.nn.softmax(hg_lb_logits.astype(jnp.float32), axis=0)
    lbs = jnp.concatenate([jnp.zeros_like(probs[0:1]), jnp.cumsum(probs, axis=0)[:-1]], axis=0)
    split_at = np.cumsum(IN_SIZES)[:-1].tolist()
    for l in range(DEPTH_2):
        hn = rmsnorm(h, norm_mix_w[l])
        proj = hn @ w_in[l]
        (q_sb, k_sb, v_sb, z_ssd, x_ssd, b_ssd, c_ssd, dt_ssd,
         q_hg, f_hg, i_hg, g_hg) = jnp.split(proj, split_at, axis=-1)
        o_sb = stick_breaking_group(q_sb, k_sb, v_sb, sb_q_norm[l], sb_k_norm[l], sb_out_norm[l], valid)
        o_ssd = ssd_group(z_ssd, x_ssd, b_ssd, c_ssd, dt_ssd, ssd_conv_w[l], ssd_conv_b[l], ssd_dt_bias[l],
                          ssd_A_log[l], ssd_D[l], ssd_norm_w[l], vmask)
        o_hg = hgrn2_group(q_hg, f_hg, i_hg, g_hg, lbs[l], hg_out_norm[l], valid)
        h = h + jnp.concatenate([o_sb, o_ssd, o_hg], axis=-1) @ w_out[l]
        hn = rmsnorm(h, norm_mlp_w[l])
        h = h + jnp.square(jax.nn.relu(hn @ w_up[l])) @ w_down[l]
    return h[:, CHUNK:]


_first_inputs = second_inputs


def second_inputs(seed=0):
    import zlib

    import numpy as np

    out = dict(_first_inputs(seed))
    spreads = {}
    factors = {'norm_mix_w': 5.819,
     'sb_q_norm': 30.956,
     'sb_k_norm': 29.336,
     'sb_out_norm': 64.0,
     'ssd_conv_b': 58.048,
     'ssd_D': 64.0,
     'ssd_norm_w': 64.0,
     'hg_out_norm': 45.586,
     'norm_mlp_w': 37.86}
    for name, (base, spread) in spreads.items():
        noise = np.random.default_rng([zlib.crc32(name.encode()), seed]).standard_normal(out[name].shape)
        drawn = base * np.exp(spread * noise) if base else spread * noise
        out[name] = jnp.asarray(drawn.astype(out[name].dtype))
    for name, factor in factors.items():
        out[name] = (out[name] * factor).astype(out[name].dtype)
    return out


_narrow_inputs = second_inputs


def second_inputs(seed=0):

    out = dict(_narrow_inputs(seed))
    wider = {'sb_out_norm': 12.0,
     'ssd_D': 12.0,
     'ssd_norm_w': 12.0,
     'hg_out_norm': 6.81,
     'norm_mlp_w': 5.59}
    for name, times in wider.items():
        mean = out[name].mean()
        out[name] = (mean + times * (out[name] - mean)).astype(out[name].dtype)
    return out


def setup_inputs(seed=0):
    out = dict(first_inputs(seed))
    for name, value in second_inputs(seed + 1).items():
        if name != "x":
            out[name + "_2"] = value
    return out


def reference(
    x, c, ctx, c_ctx, norm_g, w_ada, b_ada, w_in, w_out, diff_q_norm, diff_k_norm, lambda_q1,
    lambda_k1, lambda_q2, lambda_k2, diff_subln, gqa_q_norm, gqa_k_norm, nat_q_norm, nat_k_norm,
    nat_rpb, meta_tokens_2, hg_lb_logits_2, norm_mix_w_2, w_in_2, sb_q_norm_2, sb_k_norm_2,
    sb_out_norm_2, ssd_conv_w_2, ssd_conv_b_2, ssd_dt_bias_2, ssd_A_log_2, ssd_D_2,
    ssd_norm_w_2, hg_out_norm_2, w_out_2, norm_mlp_w_2, w_up_2, w_down_2,
):
    x = first_block(
        x, c, ctx, c_ctx, norm_g, w_ada, b_ada, w_in, w_out, diff_q_norm, diff_k_norm,
        lambda_q1, lambda_k1, lambda_q2, lambda_k2, diff_subln, gqa_q_norm, gqa_k_norm,
        nat_q_norm, nat_k_norm, nat_rpb,
    )
    return second_block(
        x, meta_tokens_2, hg_lb_logits_2, norm_mix_w_2, w_in_2, sb_q_norm_2, sb_k_norm_2,
        sb_out_norm_2, ssd_conv_w_2, ssd_conv_b_2, ssd_dt_bias_2, ssd_A_log_2, ssd_D_2,
        ssd_norm_w_2, hg_out_norm_2, w_out_2, norm_mlp_w_2, w_up_2, w_down_2,
    )


_drawn_inputs = setup_inputs


def setup_inputs(seed=0):
    import zlib

    import numpy as np

    out = dict(_drawn_inputs(seed))
    spreads = {}
    factors = {'diff_q_norm': 4.653,
     'diff_k_norm': 4.048,
     'lambda_k1': 2.908,
     'lambda_q2': 5.432,
     'lambda_k2': 6.811,
     'gqa_q_norm': 8.0,
     'gqa_k_norm': 8.0,
     'nat_q_norm': 8.0,
     'nat_k_norm': 8.0,
     'nat_rpb': 8.0,
     'ssd_D_2': 30.229}
    for name, (base, spread) in spreads.items():
        noise = np.random.default_rng([zlib.crc32(name.encode()), seed]).standard_normal(out[name].shape)
        drawn = base * np.exp(spread * noise) if base else spread * noise
        out[name] = jnp.asarray(drawn.astype(out[name].dtype))
    for name, factor in factors.items():
        out[name] = (out[name] * factor).astype(out[name].dtype)
    return out
```

```python
import math
from contextlib import ExitStack

import concourse.bass as bass
from concourse import mybir

ALU = mybir.AluOpType
ACT = mybir.ActivationFunctionType
F32 = mybir.dt.float32
AX = mybir.AxisListType.X

P = 128
D = 1024
KC = D // P
SEQ, CTX = 1024, 256
XT, CT = SEQ // P, CTX // P
NT = XT + CT
LAYERS = 2
EPS = 1e-6
NEG = -1e30
LN_EXP = "natural_log_exp_and_others"
GRID = 64
BANK = 512
SLOTS = 2
HD = 64
WIDE = 128
AH, BH, BKV, CH = 4, 6, 2, 6
DIFF_D = 32
RPB_R, RPB_C = 15, 31
RPB_N = CH * RPB_R * RPB_C
SLACK = 64
JT, JI = 14, 10

A_Q, A_V, B_Q, B_V, C_Q, C_K, C_V, C_G = 0, 512, 1024, 1536, 2048, 2432, 2816, 3200
L2T = XT + 1
S_Q, S_V, S_Z1, S_X, S_B, S_DT, H_Q, H_I = 0, 512, 1024, 1280, 1792, 2304, 2312, 2824
SBH, SSDH, SSDG, HGH = 4, 8, 2, 4
FF = 4096
LEVELS = 7

ROPE_A, ROPE_B = XT * DIFF_D, XT * HD
C1 = {"ident": P, "cosA": ROPE_A, "sinA": ROPE_A, "cosB": ROPE_B, "sinB": ROPE_B, "in": GRID, "neg": GRID}
C2 = {"ident": P, "le": P, "gt": P, "one": P, "lt": P, "ngt": P, "none": P, "valid": 1, "levels": (LEVELS + 2) * P,
      "pairs": (LEVELS + 1) * P}


def places(sizes):
    at, out = 0, {}
    for name, n in sizes.items():
        out[name] = (at, at + n)
        at += n
    return out, at


P1, N1 = places(C1)
P2, N2 = places(C2)


def constants():
    import numpy as np

    tok = np.arange(SEQ)
    row, col = (tok // GRID).astype(np.float32), (tok % GRID).astype(np.float32)

    def rope(d):
        nf = d // 4
        inv = np.float32(10000.0) ** (-np.arange(nf, dtype=np.float32) / np.float32(nf))
        ang = np.concatenate([row[:, None] * inv, col[:, None] * inv], axis=-1).astype(np.float32)
        cos, sin = np.cos(ang.astype(np.float64)), np.sin(ang.astype(np.float64))
        both = [np.concatenate([cos, cos], -1), np.concatenate([-sin, sin], -1)]
        return [a.reshape(XT, P, d).transpose(1, 0, 2).reshape(P, XT * d) for a in both]

    c = np.arange(GRID)
    c0 = np.clip(c - 8, 0, GRID - 16)
    inw = (c[None, :] >= c0[:, None]) & (c[None, :] < c0[:, None] + 16)
    inw = np.concatenate([inw, inw], 0)
    eye = np.eye(P)
    cosA, sinA = rope(DIFF_D)
    cosB, sinB = rope(HD)
    one = np.concatenate([eye, cosA, sinA, cosB, sinB, inw, np.where(inw, 0.0, NEG)], axis=1)

    j, t = np.arange(P)[:, None], np.arange(P)[None, :]
    levels, pairs = [], []
    for n in range(LEVELS):
        b = P >> (n + 1)
        mid = (t // (2 * b)) * 2 * b + b
        upper = t >= mid
        levels.append(np.where(upper, (j >= mid) & (j <= t), (j > t) & (j < mid)))
        pairs.append((j // (2 * b) == t // (2 * b)) & (j % (2 * b) < b) & (t % (2 * b) >= b))
    levels += [j <= t, j > t]
    pairs.append(j == t)
    valid = (np.arange(P) >= P - 16)[:, None]
    two = np.concatenate([eye, j <= t, j > t, np.ones((P, P)), j < t, -(1.0 * (j > t)), -np.ones((P, P)), valid]
                         + levels + pairs, axis=1)
    return np.ascontiguousarray(one, np.float32), np.ascontiguousarray(two, np.float32)


class Signal:

    def __init__(self, nc, name):
        self.sem, self.base, self.sent = nc.alloc_semaphore(name), 0, 0

    def inc(self, n=1):
        self.sent += n
        return self.sem, n

    def __call__(self, n):
        return self.sem, self.base + n


class Signals:
    def __init__(self, nc):
        self.nc, self.all = nc, {}

    def __getitem__(self, name):
        if name not in self.all:
            self.all[name] = Signal(self.nc, name)
        return self.all[name]

    def stage_ends(self):
        for s in self.all.values():
            s.base, s.sent = s.base + s.sent, 0


def spread(ap, shape, axis):
    return ap.unsqueeze(axis).to_broadcast(shape)


def chained(eng, signal):
    def step(ins):
        ins.then_inc(*signal.inc())
        eng.wait_ge(*signal(signal.sent))
    return step


class Program:
    def __init__(self, nc, io):
        self.nc, self.io, self.S = nc, io, Signals(nc)
        self.out_stored = nc.alloc_semaphore("out_stored")
        self.ring = nc.alloc_sbuf_tensor("ring", [P, SLOTS, KC * BANK], F32)
        self.ps = nc.alloc_psum_tensor("ps", [P, 8, BANK], F32)
        self.chunks = []
        self.loaded = [nc.alloc_semaphore(f"weights_loaded_{i}") for i in range(SLOTS)]
        self.spent = nc.alloc_semaphore("weights_spent")
        self.next_use = 0
        self.bias_shifted = nc.alloc_semaphore("bias_shifted")

    def view(self, i):
        k, w = self.chunks[i][1:]
        return self.ring[:, i % SLOTS, 0:k * w].rearrange("p (k n) -> p k n", k=k)

    def load(self, eng, i):
        if i >= len(self.chunks):
            return
        if i >= SLOTS:
            eng.wait_ge(self.spent, i - SLOTS + 1)
        dst, at = self.view(i), 0
        pieces = self.chunks[i][0]
        for n, src in enumerate(pieces):
            w = src.shape[2]
            eng.dma_start(dst[:, :, at:at + w], src).then_inc(self.loaded[i % SLOTS], 16)
            at += w

    def load_more(self, eng, used):
        for i in range(self.next_use, self.next_use + used):
            self.load(eng, i + SLOTS)

    def arrived(self, eng, i):
        pieces = sum(len(self.chunks[j][0]) for j in range(i % SLOTS, i + 1, SLOTS))
        eng.wait_ge(self.loaded[i % SLOTS], 16 * pieces)

    def end(self, used=0):
        self.next_use += used
        self.S.stage_ends()

    def rsqrt_act(self, act, step, out, v):
        step(act.activation(out, v, ACT.Ln))
        return act.activation(out, out, ACT.Exp, scale=-0.5)

    def rsqrt_dve(self, dve, step, e, v, t):
        step(dve.tensor_tensor(t, v, e, ALU.mult))
        step(dve.tensor_tensor(t, t, e, ALU.mult))
        step(dve.tensor_scalar(t, t, -0.5, 1.5, ALU.mult, ALU.add))
        step(dve.tensor_tensor(e, e, t, ALU.mult))


def stage_setup(pr, const, const_src, loads, rpb=None):
    nc, S = pr.nc, pr.S
    with nc.Block() as block:
        @block.sync
        def _(sp):
            if pr.next_use == 0:
                for i in range(SLOTS):
                    pr.load(sp, i)

        @block.gpsimd
        def _(pool):
            n = 0
            for dst, src in [(const[:], const_src)] + loads:
                pool.dma_start(dst, src).then_inc(*S["setup_in"].inc(16))
                n += 16
            pool.wait_ge(*S["setup_in"](n))
            if rpb is not None:
                src, scratch, zero, shifted = rpb
                pool.memset(zero[:], 0.0).then_inc(*S["zero_set"].inc())
                pool.wait_ge(*S["zero_set"](1))
                for l in range(LAYERS):
                    pool.dma_start(scratch[l:l + 1, SLACK:SLACK + RPB_N], src[l:l + 1, :]).then_inc(*S["rpb_put"].inc(16))
                    for at in (0, SLACK + RPB_N):
                        pool.dma_start(scratch[l:l + 1, at:at + SLACK], zero[0:1, :]).then_inc(*S["rpb_put"].inc(16))
                pool.wait_ge(*S["rpb_put"](16 * 3 * LAYERS))
                for l in range(LAYERS):
                    for h in range(CH):
                        at = bass.AP(tensor=scratch.tensor, offset=l * (RPB_N + 2 * SLACK) + SLACK + h * RPB_R * RPB_C + 15,
                                     ap=[[RPB_C, RPB_R], [-1, GRID], [1, GRID]])
                        pool.dma_start(shifted[l, :, h, :, :].rearrange("q r k -> r q k"), at).then_inc(pr.bias_shifted, 16)
    pr.end()


def stage_ada(pr, l, t):
    nc, S, ps = pr.nc, pr.S, pr.ps
    i0 = pr.next_use
    cols, tables = ps[:, 0, 0:64].rearrange("p (m w) -> p m w", w=2), 4
    with nc.Block() as block:
        @block.sync
        def _(sp):
            pr.load_more(sp, 6)

        @block.gpsimd
        def _(pool):
            for n, (dst, src) in enumerate(t["layer_loads"](l)):
                pool.dma_start(dst, src).then_inc(*S["layer_in"].inc(16))
            pool.wait_ge(*S["layer_in"](16 * (n + 1)))

        @block.scalar
        def _(act):
            act.activation(t["csilu"][:], t["c"][:], ACT.Silu).then_inc(*S["c_silu"].inc())
            act.wait_ge(*S["lam_sums"](2))
            act.activation(t["lam"][:, 2:4], t["lam"][:, 0:2], ACT.Exp).then_inc(*S["lam_exps"].inc())

        @block.vector
        def _(dve):
            step = chained(dve, S["dve"])
            dve.wait_ge(*S["c_silu"](1))
            for w in range(2):
                for k in range(KC):
                    ins = dve.tensor_scalar(t["crep"][:, w, k, :], t["ident"], 0.0,
                                            t["csilu"][:, 2 * k + w:2 * k + w + 1], ALU.mult, ALU.add)
            ins.then_inc(*S["c_spread"].inc())
            n_loads = len(t["layer_loads"](l))
            dve.wait_ge(*S["layer_in"](16 * n_loads))
            lv, lam = t["lamv"], t["lam"]
            for m in range(2):
                dve.tensor_tensor_reduce(t["lamj"][:, m, :], lv[:, 2 * m, :], lv[:, 2 * m + 1, :], 1.0, 0.0, ALU.mult, ALU.add,
                                         lam[:, m:m + 1]).then_inc(*S["lam_sums"].inc())
            dve.wait_ge(*S["lam_exps"](1))
            step(dve.tensor_tensor(lam[:, 4:5], lam[:, 3:4], lam[:, 2:3], ALU.subtract))
            lam_init = 0.8 - 0.6 * math.exp(-0.3 * l)
            dve.tensor_scalar(lam[:, 5:6], lam[:, 4:5], -lam_init, None, ALU.add)
            g = t["gains"]
            for n, d in ((0, DIFF_D), (2, HD), (4, HD)):
                dve.tensor_scalar(g[:, n, 0:d], g[:, n, 0:d], d ** -0.5, None, ALU.mult)
            dve.tensor_scalar(g[:, 6, :], g[:, 6, :], 1 - lam_init, None, ALU.mult)
            dve.wait_ge(pr.spent, i0 + 4)
            b = t["bada"]
            step(dve.tensor_tensor(t["sh"][:], cols[:, 0:KC, :], spread(b[:, 0:KC], [P, KC, 2], 2), ALU.add))
            step(dve.tensor_tensor(t["sc"][:], cols[:, KC:2 * KC, :], spread(b[:, KC:2 * KC], [P, KC, 2], 2), ALU.add))
            dve.scalar_tensor_tensor(out=t["sc"][:], in0=t["sc"][:], scalar=1.0, in1=spread(t["ng"][:], [P, KC, 2], 2),
                                     op0=ALU.add, op1=ALU.mult)
            for n in range(4):
                w, h = n % 2, n // 2
                if w == 0:
                    dve.wait_ge(*S["ada_gate"](h + 1))
                else:
                    dve.wait_ge(pr.spent, i0 + 5 + h)
                dve.tensor_tensor(t["gate"][:, w, h * BANK:(h + 1) * BANK], ps[:, tables + n, :],
                                  t["bgate"][:, h * BANK:(h + 1) * BANK], ALU.add)

        @block.tensor
        def _(pe):
            pe.wait_ge(*S["c_silu"](1))
            for n in range(4):
                pr.arrived(pe, i0 + n)
                w = pr.view(i0 + n)
                for m in range(4):
                    for k in range(KC):
                        mm = pe.matmul(cols[:, 4 * n + m, :], w[:, k, m * P:(m + 1) * P], t["csilu"][:, 2 * k:2 * k + 2],
                                       start=(k == 0), stop=(k == KC - 1))
                mm.then_inc(pr.spent, 1)
            for h in range(2):
                pr.arrived(pe, i0 + 4 + h)
                w = pr.view(i0 + 4 + h)
                if h == 0:
                    pe.wait_ge(*S["c_spread"](1))
                for b in range(2):
                    for k in range(KC):
                        mm = pe.matmul(ps[:, tables + 2 * h + b, :], t["crep"][:, b, k, :], w[:, k, :],
                                       start=(k == 0), stop=(k == KC - 1))
                    if b == 0:
                        mm.then_inc(*S["ada_gate"].inc())
                mm.then_inc(pr.spent, 1)
    pr.end(6)


def stage_norm(pr, sources, big, ssq, rs, out, scale, shift, ident, partial):
    nc, S, ps = pr.nc, pr.S, pr.ps
    n = len(sources)
    parts = [s for s in sources if s is not None]
    with nc.Block() as block:
        @block.sync
        def _(sp):
            for t in sorted(range(n), key=lambda t: t in partial):
                src = sources[t]
                if t in partial:
                    sp.wait_ge(*S["lead_zero"](1))
                if src is not None:
                    for rows, piece in src:
                        sp.dma_start(big[rows, t, :], piece).then_inc(*S[f"x_in_{t}"].inc(16))

        @block.scalar
        def _(act):
            step = chained(act, S["act"])
            for t, src in enumerate(sources):
                act.wait_ge(*S[f"x_in_{t}"](16 * len(src)))
                step(act.activation(pr.junk[:, 0:D], big[:, t, :], ACT.Square, accum_out=ssq[:, t:t + 1]))
            act.wait_ge(*S["v_ready"](1))
            pr.rsqrt_act(act, step, rs[:, 0:n], ssq[:, 0:n]).then_inc(*S["e_ready"].inc())
            for t in range(n):
                act.wait_ge(*S["xT_odd"](t + 1))
                for k in range(4):
                    ins = act.activation(out[:, 4 + k, t * P:(t + 1) * P], ps[:, 2 * (t % 2) + 1, k * P:(k + 1) * P],
                                         ACT.Identity, scale=scale(t, 4 + k), bias=shift(t, 4 + k))
                ins.then_inc(*S["xT_odd_used"].inc())

        def evacuate(dve, t):
            dve.wait_ge(*S["xT_even"](t + 1))
            for k in range(4):
                ins = dve.tensor_scalar(out[:, k, t * P:(t + 1) * P], ps[:, 2 * (t % 2), k * P:(k + 1) * P],
                                        scale(t, k), shift(t, k), ALU.mult, ALU.add)
            ins.then_inc(*S["xT_even_used"].inc())

        @block.vector
        def _(dve):
            step = chained(dve, S["dve"])
            dve.wait_ge(*S["act"](n))
            dve.tensor_scalar(ssq[:, 0:n], ssq[:, 0:n], 1.0 / D, EPS, ALU.mult, ALU.add).then_inc(*S["v_ready"].inc())
            dve.wait_ge(*S["e_ready"](1))
            dve.wait_ge(*S["v_ready"](1))
            pr.rsqrt_dve(dve, step, rs[:, 0:n], ssq[:, 0:n], pr.junk[:, D:D + n])
            for t in range(n):
                dve.tensor_scalar(big[:, t, :], big[:, t, :], rs[:, t:t + 1], None, ALU.mult).then_inc(*S["xn_ready"].inc())
                if t:
                    evacuate(dve, t - 1)
            evacuate(dve, n - 1)

        @block.tensor
        def _(pe):
            for t in range(n):
                pe.wait_ge(*S["xn_ready"](t + 1))
                for h, name in enumerate(("xT_even", "xT_odd")):
                    if t >= 2:
                        pe.wait_ge(*S[name + "_used"](t - 1))
                    for k in range(4):
                        mm = pe.transpose(ps[:, 2 * (t % 2) + h, k * P:(k + 1) * P],
                                          big[:, t, (4 * h + k) * P:(4 * h + k + 1) * P], ident)
                    mm.then_inc(*S[name].inc())

        @block.gpsimd
        def _(pool):
            if partial:
                for t in partial:
                    ins = pool.memset(big[:, t, :], 0.0)
                ins.then_inc(*S["lead_zero"].inc())
    pr.end()


def stage_project(pr, hT, chunks, work):
    nc, S, ps = pr.nc, pr.S, pr.ps
    i0 = pr.next_use
    units = [(c, t) for c, ch in enumerate(chunks) for t in ch["tiles"]]
    headed = [(n, c, t) for n, (c, t) in enumerate(units) if chunks[c]["heads"]]
    order = {n: m for m, (n, c, t) in enumerate(headed)}
    LAG = 2
    others = {n: m for m, n in enumerate(n for n in range(len(units)) if n not in order)}

    def bank_read(eng, n):
        eng.wait_ge(*(S["normed"](order[n] + 1) if n in order else S["parts_out"](others[n] + 1)))

    sq, nrm, rot, tmp, st = work["sq"], work["nrm"], work["rot"], work["tmp"], work["st"]
    with nc.Block() as block:
        @block.sync
        def _(sp):
            pr.load_more(sp, len(chunks))

        @block.tensor
        def _(pe):
            def transposes(m):
                n, c, t = headed[m]
                pe.wait_ge(*S["rotated"](m + 1))
                if m >= 2:
                    pe.wait_ge(*S["qkT_kept"](m - 1))
                blocks = chunks[c]["width_heads"] // P
                for b in range(blocks):
                    mm = pe.transpose(ps[:, 2 + m % 2, b * P:(b + 1) * P], rot[:, m % 2, b * P:(b + 1) * P], work["ident"])
                mm.then_inc(*S["qkT_ready"].inc())

            done = 0
            for n, (c, t) in enumerate(units):
                if t == chunks[c]["tiles"][0]:
                    pr.arrived(pe, i0 + c)
                w = pr.view(i0 + c)
                if n >= 2:
                    bank_read(pe, n - 2)
                width = w.shape[2]
                last = t == chunks[c]["tiles"][-1]
                for k in range(KC):
                    mm = pe.matmul(ps[:, n % 2, 0:width], hT[:, k, t * P:(t + 1) * P], w[:, k, :],
                                   start=(k == 0), stop=(k == KC - 1))
                mm.then_inc(*S["proj_done"].inc())
                if last:
                    pe.wait_ge(*S["proj_done"](n + 1))
                    pe.sem_inc(pr.spent, 1)
                while done < len(headed) and headed[done][0] <= n - LAG:
                    transposes(done)
                    done += 1
            while done < len(headed):
                transposes(done)
                done += 1

        @block.scalar
        def _(act):
            step = chained(act, S["act"])

            if chunks[0]["heads"]:
                act.preload_act_table_set(LN_EXP)

            def keep(m):
                n, c, t = headed[m]
                act.wait_ge(*S["qkT_ready"](m + 1))
                blocks = chunks[c]["width_heads"] // P
                dst = chunks[c]["dst"]
                act.activation(dst[:, chunks[c]["b0"]:chunks[c]["b0"] + blocks, t * P:(t + 1) * P],
                               ps[:, 2 + m % 2, 0:blocks * P].rearrange("p (b n) -> p b n", b=blocks),
                               ACT.Copy).then_inc(*S["qkT_kept"].inc())

            kept = 0
            for n, (c, t) in enumerate(units):
                ch = chunks[c]
                act.wait_ge(*S["proj_done"](n + 1))
                if ch["heads"]:
                    m, nh = order[n], ch["n_heads"]
                    if m >= 2:
                        act.wait_ge(*S["v_ready"](m - 1))
                    act.activation(sq[:, m % 2, 0:ch["width_heads"]], ps[:, n % 2, 0:ch["width_heads"]],
                                   ACT.Square).then_inc(*S["squares"].inc())
                for kind, lo, hi, dst in ch["parts"]:
                    src, d = ps[:, n % 2, lo:hi], dst(t)
                    if d is None:
                        continue
                    if len(d.shape) == 3:
                        src = src.rearrange("p (h d) -> p h d", h=d.shape[1])
                    ins = act.activation(d, src, {"copy": ACT.Copy, "silu": ACT.Silu}[kind])
                if not ch["heads"]:
                    ins.then_inc(*S["parts_out"].inc())
                if ch["heads"]:
                    act.wait_ge(*S["v_ready"](m + 1))
                    pr.rsqrt_act(act, step, st[:, m % 2, 1, 0:nh], st[:, m % 2, 0, 0:nh]).then_inc(*S["e_ready"].inc())
                while kept < len(headed) and headed[kept][0] <= n - LAG:
                    keep(kept)
                    kept += 1
            while kept < len(headed):
                keep(kept)
                kept += 1

        @block.vector
        def _(dve):
            step = chained(dve, S["dve"])
            if "scale_of" in work:
                g, by = work["scale_of"]
                step(dve.tensor_scalar(g, g, by, None, ALU.mult))
            for m, (n, c, t) in enumerate(headed):
                ch = chunks[c]
                nh, d, w = ch["n_heads"], ch["dim"], ch["width_heads"]
                v, e, x = (st[:, m % 2, i, 0:nh] for i in range(3))
                dve.wait_ge(*S["squares"](m + 1))
                if m >= 2:
                    dve.wait_ge(*S["e_ready"](m - 1))
                step(dve.reduce_sum(v, sq[:, m % 2, 0:w].rearrange("p (h d) -> p h d", d=d), AX))
                dve.tensor_scalar(v, v, 1.0 / d, EPS, ALU.mult, ALU.add).then_inc(*S["v_ready"].inc())
                dve.wait_ge(*S["v_ready"](m + 1))
                dve.wait_ge(*S["e_ready"](m + 1))
                pr.rsqrt_dve(dve, step, e, v, x)
                if m >= 2:
                    dve.wait_ge(*S["rotated"](m - 1))
                dve.tensor_tensor(nrm[:, m % 2, 0:w].rearrange("p (h d) -> p h d", d=d),
                                  ps[:, n % 2, 0:w].rearrange("p (h d) -> p h d", d=d),
                                  spread(e, [P, nh, d], 2), ALU.mult).then_inc(*S["normed"].inc())

        @block.gpsimd
        def _(pool):
            step = chained(pool, S["pool"])
            if work.get("ones_of") is not None:
                for ones in work["ones_of"]:
                    pool.memset(ones, 1.0)
            for m, (n, c, t) in enumerate(headed):
                ch = chunks[c]
                pool.wait_ge(*S["normed"](m + 1))
                if m >= 2:
                    pool.wait_ge(*S["qkT_ready"](m - 1))
                d, w, h = ch["dim"], ch["width_heads"], ch["dim"] // 2
                nh = ch["n_heads"]
                x = nrm[:, m % 2, 0:w].rearrange("p (h d) -> p h d", d=d)
                roped = ch["rope"] is not None and t < XT
                outs = [(g, a, b, *f(x[:, a:b, :], rot[:, m % 2, a * d:b * d])) for g, a, b, f in ch["gain"]]
                for g, a, b, src, dst in outs:
                    gain = spread(g, [P, b - a, d], 1)
                    ins = pool.tensor_tensor(x[:, a:b, :] if roped else dst, x[:, a:b, :] if roped else src,
                                             gain if roped or len(dst.shape) == 3
                                             else gain.rearrange("p (u v) d -> p u v d", u=dst.shape[1]), ALU.mult)
                if not roped:
                    ins.then_inc(*S["rotated"].inc())
                    continue
                step(ins)
                cos, sin = (r[:, t, :] for r in ch["rope"])
                tm = tmp[:, 0:w].rearrange("p (h d) -> p h d", d=d)
                pool.tensor_tensor(tm[:, :, 0:h], x[:, :, h:d], spread(sin[:, 0:h], [P, nh, h], 1), ALU.mult)
                step(pool.tensor_tensor(tm[:, :, h:d], x[:, :, 0:h], spread(sin[:, h:d], [P, nh, h], 1), ALU.mult))
                step(pool.tensor_tensor(x, x, spread(cos, [P, nh, d], 1), ALU.mult))
                for g, a, b, src, dst in outs:
                    f = [q for q in ch["gain"] if q[1] == a][0][3]
                    ins = pool.tensor_tensor(dst, src, f(tm[:, a:b, :], rot[:, m % 2, a * d:b * d])[0], ALU.add)
                ins.then_inc(*S["rotated"].inc())
    pr.end(len(chunks))


def plain(src, flat):
    return src, flat.rearrange("p (h d) -> p h d", d=src.shape[2])


def kv_halves(src, flat):
    return (src.rearrange("p (g b) d -> p g b d", g=BKV), flat.rearrange("p (b g d) -> p g b d", g=BKV, d=HD))


def stage_attend(pr, units, qk, V, Pb, Ssb, PT, small, ident, post, bias=None, prepare=None, finish=None):
    nc, S, ps = pr.nc, pr.S, pr.ps
    n = len(units)
    TB = 6
    groups = [[u["blocks"][a:a + 4] for a in range(0, len(u["blocks"]), 4)] for u in units]
    nb = [len(u["banks"]) for u in units]
    first_bank = [sum(nb[:i]) for i in range(n + 1)]
    ng = [len(g) for g in groups]
    first_group = [sum(ng[:i]) for i in range(n + 1)]
    by_act = [g == 1 for i in range(n) for g in range(ng[i])]
    act_copies = [sum(by_act[:j + 1]) for j in range(len(by_act))]

    def copied(eng, j):
        if by_act[j]:
            eng.wait_ge(*S["pT_kept_act"](act_copies[j]))
        else:
            eng.wait_ge(*S["pT_kept_dve"](j + 1 - act_copies[j]))

    def o_bank(i):
        return ps[:, 3 * (i % 2) + 2, BANK - WIDE:BANK]

    with nc.Block() as block:
        @block.sync
        def _(sp):
            if prepare:
                prepare["sync"](sp)

        @block.gpsimd
        def _(pool):
            if prepare:
                prepare["gpsimd"](pool)

        @block.tensor
        def _(pe):
            def scores(i, b):
                u = units[i]
                bank = 3 * (i % 2) + b
                if i >= 2:
                    pe.wait_ge(*S["exps"](first_bank[i - 2] + min(b + 1, nb[i - 2])))
                    if b == 2:
                        pe.wait_ge(*S["o_used"](i - 1))
                q = qk[u["rows"], u["qb"], u["qt"] * P:(u["qt"] + 1) * P]
                for piece in u["banks"][b]:
                    mm = pe.matmul(ps[:, bank, piece["at"]:piece["at"] + piece["w"]], q,
                                   qk[u["rows"], u["kb"], piece["key"]:piece["key"] + piece["w"]], start=True, stop=True)
                mm.then_inc(*S["scored"].inc())

            def transposes(i, g):
                j = first_group[i] + g
                if g == 0:
                    pe.wait_ge(*S["exps"](first_bank[i + 1]))
                if j >= 2:
                    copied(pe, j - 2)
                for b, (col, key) in enumerate(groups[i][g]):
                    mm = pe.transpose(ps[:, TB + j % 2, b * P:(b + 1) * P], Pb[:, i % 2, col:col + P], ident)
                mm.then_inc(*S["pT_ready"].inc())

            def weighted(i):
                u = units[i]
                if i >= 2:
                    pe.wait_ge(*S["o_used"](i - 1))
                blocks = u["blocks"]
                for b, (col, key) in enumerate(blocks):
                    if b % 4 == 0:
                        copied(pe, first_group[i] + b // 4)
                    v = V[:, key // P, u["vh"] * (HD + 1):u["vh"] * (HD + 1) + WIDE]
                    mm = pe.matmul(o_bank(i), PT[:, i % 2, b, :], v, start=(b == 0), stop=(b == len(blocks) - 1))
                mm.then_inc(*S["o_ready"].inc())

            for b in range(nb[0]):
                scores(0, b)
            for i in range(n):
                for s in range(max(ng[i], nb[i + 1] if i + 1 < n else 0)):
                    if i + 1 < n and s < nb[i + 1]:
                        scores(i + 1, s)
                    if s < ng[i]:
                        transposes(i, s)
                weighted(i)

        def keep_group(eng, i, g):
            j = first_group[i] + g
            eng.wait_ge(*S["pT_ready"](j + 1))
            if i >= 2 and g <= 1:
                eng.wait_ge(*S["o_ready"](i - 1))
            k = len(groups[i][g])
            dst, src = PT[:, i % 2, 4 * g:4 * g + k, :], ps[:, TB + j % 2, 0:k * P].rearrange("p (b n) -> p b n", b=k)
            if not by_act[j]:
                eng.tensor_copy(dst, src).then_inc(*S["pT_kept_dve"].inc())
            else:
                eng.activation(dst, src, ACT.Copy).then_inc(*S["pT_kept_act"].inc())

        @block.scalar
        def _(act):
            if prepare and "scalar" in prepare:
                prepare["scalar"](act)

            def exps(i):
                u = units[i]
                act.wait_ge(*S["neg_max"](i + 1))
                for b, bank in enumerate(u["banks"]):
                    for piece in bank:
                        src = ps[:, 3 * (i % 2) + b, piece["at"]:piece["at"] + piece["w"]]
                        if piece.get("bias"):
                            src = Ssb[:, i % 2, piece["at"] + b * BANK:piece["at"] + b * BANK + piece["w"]]
                        col = piece["col"]
                        if b == 0 and i >= 2:
                            act.wait_ge(*S["pT_ready"](first_group[i - 1]))
                        ins = act.activation(Pb[:, i % 2, col:col + piece["w"]], src, ACT.Exp,
                                             bias=small[:, i % 2, 8:9])
                    ins.then_inc(*S["exps"].inc())

            exps(0)
            for i in range(n):
                if ng[i] > 1:
                    keep_group(act, i, 1)
                if i + 1 < n:
                    exps(i + 1)

        @block.vector
        def _(dve):
            step = chained(dve, S["dve"])
            if prepare and "vector" in prepare:
                prepare["vector"](dve, step)

            def maxima(i, b):
                u = units[i]
                m = sum(len(bank) for bank in u["banks"][:b])
                if i >= 2 and b == 0:
                    dve.wait_ge(*S["exps"](first_bank[i - 1]))
                dve.wait_ge(*S["scored"](first_bank[i] + b + 1))
                for piece in u["banks"][b]:
                    src = ps[:, 3 * (i % 2) + b, piece["at"]:piece["at"] + piece["w"]]
                    if piece.get("bias"):
                        at = piece["at"] + b * BANK
                        ins = dve.tensor_tensor_reduce(Ssb[:, i % 2, at:at + piece["w"]], src, bias(u, piece), 1.0, -3e38,
                                                       ALU.add, ALU.max, small[:, i % 2, m:m + 1])
                    else:
                        ins = dve.reduce_max(small[:, i % 2, m:m + 1], src, AX)
                    m += 1
                if b == nb[i] - 1:
                    step(ins)
                    dve.tensor_reduce(small[:, i % 2, 8:9], small[:, i % 2, 0:m], AX, ALU.max,
                                      negate=True).then_inc(*S["neg_max"].inc())

            def evacuate(i):
                dve.wait_ge(*S["o_ready"](i + 1))
                post(dve, step, units[i], o_bank(i), i).then_inc(*S["o_used"].inc())

            for b in range(nb[0]):
                maxima(0, b)
            for i in range(n):
                if i >= 1:
                    evacuate(i - 1)
                for b in range(max(ng[i], nb[i + 1] if i + 1 < n else 0)):
                    if i + 1 < n and b < nb[i + 1]:
                        maxima(i + 1, b)
                    if b < ng[i] and b != 1:
                        keep_group(dve, i, b)
            evacuate(n - 1)
            if finish:
                dve.wait_ge(*S["o_used"](n))
                finish(dve, step)
    pr.end()


def stage_head_norm(pr, o, tiles, heads, gain, st, y, sq, gain_is_wide, dim=HD):
    nc, S = pr.nc, pr.S
    nh = tiles * heads
    w = heads * dim
    v, e, x = (st[:, i, 0:nh] for i in range(3))
    with nc.Block() as block:
        @block.scalar
        def _(act):
            step = chained(act, S["act"])
            for t in range(tiles):
                if t >= 2:
                    act.wait_ge(*S["summed"](t - 1))
                act.activation(sq[:, t % 2, 0:w], o(t), ACT.Square).then_inc(*S["squares"].inc())
            act.wait_ge(*S["v_ready"](1))
            pr.rsqrt_act(act, step, e, v).then_inc(*S["e_ready"].inc())

        @block.vector
        def _(dve):
            step = chained(dve, S["dve"])
            for t in range(tiles):
                dve.wait_ge(*S["squares"](t + 1))
                dve.reduce_sum(v[:, t * heads:(t + 1) * heads], sq[:, t % 2, 0:w].rearrange("p (h d) -> p h d", d=dim),
                               AX).then_inc(*S["summed"].inc())
            dve.wait_ge(*S["summed"](tiles))
            dve.tensor_scalar(v, v, 1.0 / dim, EPS, ALU.mult, ALU.add).then_inc(*S["v_ready"].inc())
            dve.wait_ge(*S["e_ready"](1))
            dve.wait_ge(*S["v_ready"](1))
            pr.rsqrt_dve(dve, step, e, v, x)
            for t in range(tiles):
                s = sq[:, t % 2, 0:w].rearrange("p (h d) -> p h d", d=dim)
                if t < 2:
                    dve.wait_ge(*S["squares"](tiles))
                else:
                    dve.wait_ge(*S["gained"](t - 1))
                ot = o(t).rearrange("p (h d) -> p h d", d=dim)
                dve.tensor_tensor(s, ot, spread(e[:, t * heads:(t + 1) * heads], [P, heads, dim], 2),
                                  ALU.mult).then_inc(*S["scaled"].inc())
                if y is not None:
                    dve.wait_ge(*S["scaled"](t + 1))
                    dve.tensor_tensor(y(t), sq[:, t % 2, 0:w], y(t), ALU.mult).then_inc(*S["gated"].inc())

        @block.gpsimd
        def _(pool):
            for t in range(tiles):
                dst = y(t) if y is not None else o(t)
                pool.wait_ge(*S["gated" if y is not None else "scaled"](t + 1))
                src = dst if y is not None else sq[:, t % 2, 0:w]
                g = gain if gain_is_wide else spread(gain, [P, heads, dim], 1)
                if not gain_is_wide:
                    dst, src = (a.rearrange("p (h d) -> p h d", d=dim) for a in (dst, src))
                pool.tensor_tensor(dst, src, g, ALU.mult).then_inc(*S["gained"].inc())
    pr.end()


def stage_out(pr, tiles, Y, yT, x_rows, dst_rows, gate, xt, res, ident):
    nc, S, ps = pr.nc, pr.S, pr.ps
    i0 = pr.next_use
    n = len(tiles)
    with nc.Block() as block:
        @block.sync
        def _(sp):
            for m, t in enumerate(tiles[0:2]):
                sp.dma_start(xt[:, m % 2, :], x_rows(t)).then_inc(*S[f"x_in_{m % 2}"].inc(16))
            for m, t in enumerate(tiles):
                sp.wait_ge(*S["x_new"](m + 1))
                sp.dma_start(dst_rows(t), res[:, m % 2, :]).then_inc(*S[f"x_out_{m % 2}"].inc(16))
                if m + 2 < n:
                    sp.dma_start(xt[:, m % 2, :], x_rows(tiles[m + 2])).then_inc(*S[f"x_in_{m % 2}"].inc(16))
            for m in range(2):
                sp.wait_ge(*S[f"x_out_{m}"](16 * n // 2))
            pr.load_more(sp, 2)

        @block.tensor
        def _(pe):
            def turn(m):
                t = tiles[m]
                for h in range(2):
                    if m >= 1:
                        pe.wait_ge(*S["yT_kept"](2 * (m - 1) + h + 1))
                    for k in range(4):
                        mm = pe.transpose(ps[:, h, k * P:(k + 1) * P], Y[:, t, (4 * h + k) * P:(4 * h + k + 1) * P], ident)
                    mm.then_inc(*S["yT_ready"].inc())

            turn(0)
            for m, t in enumerate(tiles):
                if m + 1 < n:
                    turn(m + 1)
                pe.wait_ge(*S["yT_kept"](2 * m + 2))
                if m >= 2:
                    pe.wait_ge(*S["x_new"](m - 1))
                for h in range(2):
                    if m == 0:
                        pr.arrived(pe, i0 + h)
                    w = pr.view(i0 + h)
                    for k in range(KC):
                        mm = pe.matmul(ps[:, 2 + 2 * (m % 2) + h, :], yT[:, m % 2, k, :], w[:, k, :],
                                       start=(k == 0), stop=(k == KC - 1))
                    mm.then_inc(*S["proj_done"].inc())
            for h in range(2):
                pe.wait_ge(*S["proj_done"](2 * n))
                pe.sem_inc(pr.spent, 1)

        @block.scalar
        def _(act):
            for m in range(n):
                for h in range(2):
                    act.wait_ge(*S["yT_ready"](2 * m + h + 1))
                    if m >= 2:
                        act.wait_ge(*S["proj_done"](2 * (m - 1)))
                    act.activation(yT[:, m % 2, 4 * h:4 * h + 4, :], ps[:, h, :].rearrange("p (k n) -> p k n", k=4),
                                   ACT.Copy).then_inc(*S["yT_kept"].inc())

        @block.vector
        def _(dve):
            step = chained(dve, S["dve"])
            for m, t in enumerate(tiles):
                dve.wait_ge(*S["proj_done"](2 * m + 2))
                if m >= 2:
                    dve.wait_ge(*S[f"x_out_{m % 2}"](16 * (m // 2)))
                pv = ps[:, 2 + 2 * (m % 2):4 + 2 * (m % 2), :]
                r = res[:, m % 2, :].rearrange("p (h n) -> p h n", h=2)
                g = gate(t)
                if g is not None:
                    step(dve.tensor_tensor(r, pv, g.rearrange("p (h n) -> p h n", h=2), ALU.mult))
                    src = r
                else:
                    src = pv
                dve.wait_ge(*S[f"x_in_{m % 2}"](16 * (m // 2 + 1)))
                dve.tensor_tensor(r, src, xt[:, m % 2, :].rearrange("p (h n) -> p h n", h=2), ALU.add).then_inc(*S["x_new"].inc())
    pr.end(2)


def stage_mlp_half(pr, hT, hid, base, x_rows, out_rows, xt, res, out_sem, first):
    nc, S, ps = pr.nc, pr.S, pr.ps
    i0 = pr.next_use
    NU, ND = FF // BANK, FF // BANK
    TT = BANK // P
    with nc.Block() as block:
        @block.sync
        def _(sp):
            for t in range(2):
                sp.dma_start(xt[:, t, :], x_rows(t)).then_inc(*S[f"x_in_{t}"].inc(16))
            pr.load_more(sp, NU + ND)
            for t in range(TT):
                sp.wait_ge(*S["x_new"](t + 1))
                sp.dma_start(out_rows(t), res[:, t % 2, :]).then_inc(out_sem, 16)
                if t + 2 < TT:
                    sp.dma_start(xt[:, t % 2, :], x_rows(t + 2)).then_inc(*S[f"x_in_{t % 2}"].inc(16))
            sp.wait_ge(out_sem, first + 16 * TT)

        @block.tensor
        def _(pe):
            for c in range(NU):
                pr.arrived(pe, i0 + c)
                w = pr.view(i0 + c)
                for m in range(4):
                    j = 4 * c + m
                    if j >= 2:
                        pe.wait_ge(*S["hidden_read"](j - 1))
                    for k in range(KC):
                        mm = pe.matmul(ps[:, j % 2, :], w[:, k, m * P:(m + 1) * P], hT[:, k, base:base + BANK],
                                       start=(k == 0), stop=(k == KC - 1))
                    mm.then_inc(*S["hidden_up"].inc())
                pe.wait_ge(*S["hidden_up"](4 * c + 4))
                pe.sem_inc(pr.spent, 1)
            pe.wait_ge(*S["hidden_read"](4 * NU))
            for c in range(ND):
                pr.arrived(pe, i0 + NU + c)
                w = pr.view(i0 + NU + c)
                for k in range(4):
                    j = 4 * c + k
                    pe.wait_ge(*S["hidden_kept"](j + 1))
                    for t in range(TT):
                        for h in range(2):
                            mm = pe.matmul(ps[:, 2 * t + h, :], hid[:, j, t * P:(t + 1) * P], w[:, k, h * BANK:(h + 1) * BANK],
                                           start=(j == 0), stop=(j == 4 * ND - 1))
                mm.then_inc(*S["down"].inc())
                pe.wait_ge(*S["down"](c + 1))
                pe.sem_inc(pr.spent, 1)

        @block.scalar
        def _(act):
            for j in range(4 * NU):
                act.wait_ge(*S["hidden_up"](j + 1))
                act.activation(hid[:, j, :], ps[:, j % 2, :], ACT.Relu).then_inc(*S["hidden_read"].inc())

        @block.vector
        def _(dve):
            for j in range(4 * NU):
                dve.wait_ge(*S["hidden_read"](j + 1))
                dve.tensor_tensor(hid[:, j, :], hid[:, j, :], hid[:, j, :], ALU.mult).then_inc(*S["hidden_kept"].inc())
            dve.wait_ge(*S["down"](ND))
            for t in range(TT):
                dve.wait_ge(*S[f"x_in_{t % 2}"](16 * (t // 2 + 1)))
                if t >= 2:
                    dve.wait_ge(out_sem, first + 16 * t)
                dve.tensor_tensor(res[:, t % 2, :].rearrange("p (h n) -> p h n", h=2), ps[:, 2 * t:2 * t + 2, :],
                                  xt[:, t % 2, :].rearrange("p (h n) -> p h n", h=2), ALU.add).then_inc(*S["x_new"].inc())
    pr.end(NU + ND)


def stage_stick(pr, qk, V, Y, c, buf):
    nc, S, ps = pr.nc, pr.S, pr.ps
    steps = [(qt, kt) for qt in range(1, L2T) for kt in range(qt, -1, -1)]
    n = len(steps)
    W = SBH * P
    LB, OB = 4, 6
    mag, sp, sn, w, acc = buf["mag"], buf["sp"], buf["sn"], buf["w"], buf["acc"]

    def z_of(i):
        b = 2 * (i % 2)
        return ps[:, b:b + 2, 0:2 * P]

    def split(ap):
        return ap.rearrange("p (a n) -> p a n", a=2)

    def wide(ap):
        return spread(ap, [P, SBH, P], 1)

    def by_head(ap):
        return ap.rearrange("p (h n) -> p h n", h=SBH)

    with nc.Block() as block:
        @block.tensor
        def _(pe):
            def scores(i):
                qt, kt = steps[i]
                if i >= 2:
                    pe.wait_ge(*S["minus_log_sig"](i - 1))
                for half in range(2):
                    for b in range(2):
                        r = slice(64 * half, 64 * half + 64)
                        mm = pe.matmul(ps[:, 2 * (i % 2) + half, b * P:(b + 1) * P], qk[r, 2 + b, kt * P:(kt + 1) * P],
                                       qk[r, b, qt * P:(qt + 1) * P], start=True, stop=True)
                mm.then_inc(*S["scored"].inc())

            def suffix(i):
                qt, kt = steps[i]
                pe.wait_ge(*S["softplus"](i + 1))
                if i >= 2:
                    pe.wait_ge(*S["log_w"](i - 1))
                pe.matmul(ps[:, LB + i % 2, :], c["ngt"], sp[:, i % 2, :], start=True, stop=(kt == qt)).then_inc(*S["suffixed_0"].inc())
                if kt != qt:
                    pe.wait_ge(*S["later_sum"](i))
                    pe.matmul(ps[:, LB + i % 2, :], c["none"], acc[:], start=False, stop=True)\
                      .then_inc(*S["suffixed_1"].inc())

            def weighted(i):
                qt, kt = steps[i]
                pe.wait_ge(*S["w_ready"](i + 1))
                if kt == qt and qt > 1:
                    pe.wait_ge(*S["o_used"](qt - 1))
                for h in range(SBH):
                    at = (h % 2) * 2 * P + (h // 2) * P
                    mm = pe.matmul(ps[:, OB, h * P:h * P + WIDE], w[:, i % 2, at:at + P], V[:, kt, h * HD:h * HD + WIDE],
                                   start=(kt == qt and h == 0), stop=(kt == 0), skip_group_check=True)
                mm.then_inc(*S["w_used"].inc())

            scores(0)
            for i in range(n):
                if i + 1 < n:
                    scores(i + 1)
                suffix(i)
                if i >= 1:
                    weighted(i - 1)
            weighted(n - 1)

        firsts = [i for i, (qt, kt) in enumerate(steps) if qt == kt]
        more = [sum(1 for x in steps[:i] if x[0] != x[1]) for i in range(n + 1)]

        def suffixed(eng, i):
            eng.wait_ge(*S["suffixed_0"](i + 1))
            if more[i + 1]:
                eng.wait_ge(*S["suffixed_1"](more[i + 1]))

        @block.scalar
        def _(act):
            act.preload_act_table_set(LN_EXP)
            step = chained(act, S["act"])

            def tails(i):
                act.wait_ge(*S["scored"](i + 1))
                if i >= 2:
                    act.wait_ge(*S["minus_log_sig"](i - 1))
                m = mag[:, i % 2, :]
                step(act.activation(split(m), z_of(i), ACT.Abs))
                step(act.activation(m, m, ACT.Exp, scale=-1.0))
                act.activation(m, m, ACT.Ln, bias=1.0).then_inc(*S["log1p"].inc())

            tails(0)
            for i in range(n):
                if i + 1 < n:
                    tails(i + 1)
                act.wait_ge(*S["log_w"](i + 1))
                if i >= 2:
                    act.wait_ge(*S["w_used"](i - 1))
                if steps[i][0] == steps[i][1]:
                    act.activation(w[:, i % 2, :], sn[:, i % 2, :], ACT.Exp).then_inc(*S["w_raw"].inc())
                else:
                    act.activation(w[:, i % 2, :], sn[:, i % 2, :], ACT.Exp).then_inc(*S["w_ready"].inc())

        def keep(dve, i):
            dve.wait_ge(*S["w_used"](i + 1))
            dve.tensor_copy(Y[:, steps[i][0] - 1, 0:SBH * HD].rearrange("p (h d) -> p h d", h=SBH),
                            ps[:, OB, :].rearrange("p (h d) -> p h d", h=SBH)[:, :, 0:HD]).then_inc(*S["o_used"].inc())

        @block.vector
        def _(dve):
            step = chained(dve, S["dve"])
            for i, (qt, kt) in enumerate(steps):
                diag = qt == kt
                m, s, t = mag[:, i % 2, :], sp[:, i % 2, :], sn[:, i % 2, :]
                dve.wait_ge(*S["log1p"](i + 1))
                if i >= 2:
                    dve.wait_ge(*S["suffixed_0"](i - 1))
                    dve.wait_ge(*S["later_sum"](i - 1))
                raw = dve.scalar_tensor_tensor(out=split(s), in0=z_of(i), scalar=0.0, in1=split(m), op0=ALU.max, op1=ALU.add)
                step(raw)
                if i >= 2:
                    dve.wait_ge(*S["w_used"](i - 1))
                dve.tensor_tensor(split(t), split(s), z_of(i), ALU.subtract).then_inc(*S["minus_log_sig"].inc())
                dve.wait_ge(*S["minus_log_sig"](i + 1))
                if diag:
                    dve.tensor_tensor(by_head(s), by_head(s), wide(c["lt"]), ALU.mult).then_inc(*S["softplus"].inc())
                else:
                    dve.sem_inc(*S["softplus"].inc())
                suffixed(dve, i)
                dve.tensor_tensor(t, ps[:, LB + i % 2, :], t, ALU.subtract).then_inc(*S["log_w"].inc())
                if diag:
                    dve.wait_ge(*S["w_raw"](qt))
                    dve.tensor_tensor(by_head(w[:, i % 2, :]), by_head(w[:, i % 2, :]), wide(c["lt"]), ALU.mult)\
                       .then_inc(*S["w_ready"].inc())
                if diag and i:
                    keep(dve, i - 1)
            keep(dve, n - 1)

        @block.gpsimd
        def _(pool):
            for i, (qt, kt) in enumerate(steps):
                pool.wait_ge(*S["softplus"](i + 1))
                if i >= 1:
                    pool.wait_ge(*S["later_sum"](i))
                if more[i + 1]:
                    pool.wait_ge(*S["suffixed_1"](more[i + 1]))
                s = sp[:, i % 2, :]
                if qt == kt:
                    ins = pool.tensor_copy(acc[:], s)
                else:
                    ins = pool.tensor_tensor(acc[:], acc[:], s, ALU.add)
                ins.then_inc(*S["later_sum"].inc())
    pr.end()


def stage_conv(pr, hT, convT, raw, cw, cb):
    nc, S, ps = pr.nc, pr.S, pr.ps
    i0 = pr.next_use
    NB, TW, PARTS = 8, 3 * P, L2T // 3
    L = L2T * P
    with nc.Block() as block:
        @block.sync
        def _(sp):
            pr.load_more(sp, 2)

        @block.tensor
        def _(pe):
            for b in range(NB):
                if b % 4 == 0:
                    pr.arrived(pe, i0 + b // 4)
                w = pr.view(i0 + b // 4)
                for q in range(PARTS):
                    j = b * PARTS + q
                    if j >= 4:
                        pe.wait_ge(*S["raw_kept"](j - 3))
                    for k in range(KC):
                        mm = pe.matmul(ps[:, j % 4, 0:TW], w[:, k, (b % 4) * P:(b % 4 + 1) * P], hT[:, k, q * TW:(q + 1) * TW],
                                       start=(k == 0), stop=(k == KC - 1))
                    mm.then_inc(*S["proj_done"].inc())
                if b % 4 == 3:
                    pe.wait_ge(*S["proj_done"]((b + 1) * PARTS))
                    pe.sem_inc(pr.spent, 1)

        @block.gpsimd
        def _(pool):
            pool.memset(raw[:, :, 0:3], 0.0).then_inc(*S["halo_zero"].inc())

        @block.scalar
        def _(act):
            act.wait_ge(*S["halo_zero"](1))
            def start(b):
                for q in range(PARTS):
                    j = b * PARTS + q
                    act.wait_ge(*S["proj_done"](j + 1))
                    if b >= 2:
                        act.wait_ge(*S["conv_done"](b - 1))
                    act.activation(raw[:, b % 2, 3 + q * TW:3 + (q + 1) * TW], ps[:, j % 4, 0:TW], ACT.Copy)\
                       .then_inc(*S["raw_kept"].inc())
                act.wait_ge(*S["raw_kept"]((b + 1) * PARTS))
                act.activation(convT[:, b, :], raw[:, b % 2, 3:3 + L], ACT.Identity, scale=cw[:, b, 3:4],
                               bias=cb[:, b:b + 1]).then_inc(*S["conv_begun"].inc())

            start(0)
            for b in range(NB):
                if b + 1 < NB:
                    start(b + 1)
                act.wait_ge(*S["conv_done"](b + 1))
                act.activation(convT[:, b, :], convT[:, b, :], ACT.Silu)

        @block.vector
        def _(dve):
            step = chained(dve, S["dve"])
            for b in range(NB):
                dve.wait_ge(*S["conv_begun"](b + 1))
                for j in range(3):
                    ins = dve.scalar_tensor_tensor(out=convT[:, b, :], in0=raw[:, b % 2, j:j + L], scalar=cw[:, b, j:j + 1],
                                                   in1=convT[:, b, :], op0=ALU.mult, op1=ALU.add)
                    if j < 2:
                        step(ins)
                ins.then_inc(*S["conv_done"].inc())
    pr.end(2)


def stage_ssd(pr, convT, Y, dt, par, c, b_):
    nc, S, ps = pr.nc, pr.S, pr.ps
    H, NH = SSDH, L2T * SSDH
    aU, xt, Bt, W, xdt, xend, st, cbm, E, t1, t2 = (b_[k] for k in ("aU", "xt", "Bt", "W", "xdt", "xend", "state", "cbm", "E",
                                                                   "t1", "t2"))
    sc = b_["sc"]
    dtb, alog, dskip = par[:, 0:8], par[:, 8:16], par[:, 16:24]
    GW = SSDH // SSDG * HD

    def heads(ap):
        return ap.rearrange("p (h d) -> p h d", d=HD)

    with nc.Block() as block:
        @block.scalar
        def _(act):
            step = chained(act, S["act"])
            act.activation(par[:, 24:32], alog, ACT.Exp).then_inc(*S["a_exp"].inc())
            act.wait_ge(*S["dt_biased"](1))
            flat = dt[:].rearrange("p t h -> p (t h)")
            step(act.activation(sc[:, 0, :], flat, ACT.Abs))
            step(act.activation(sc[:, 0, :], sc[:, 0, :], ACT.Exp, scale=-1.0))
            act.activation(sc[:, 0, :], sc[:, 0, :], ACT.Ln, bias=1.0).then_inc(*S["log1p"].inc())
            act.wait_ge(*S["decay_sums"](1))
            act.activation(E[:], ps[:, 0, 0:3 * NH].rearrange("p (a n) -> p a n", a=3), ACT.Exp).then_inc(*S["decays"].inc())
            for i in range(L2T):
                act.wait_ge(*S["turned"](i + 1))
                if i >= 2:
                    if i >= 3:
                        act.wait_ge(*S["y_out"](i - 2))
                    act.wait_ge(*S["state_sum"](i - 1))
                act.activation(xt[:, i % 2, :], ps[:, 0, :], ACT.Copy)
                act.activation(Bt[:, i % 2, :], ps[:, 1, 0:2 * P], ACT.Copy).then_inc(*S["xB_kept"].inc())
                if i >= 1:
                    act.wait_ge(*S["segments"](i))
                    if i >= 2:
                        act.wait_ge(*S["diag_done"](i - 1))
                    for g in range(2):
                        ins = act.activation(W[:, 4 * g:4 * g + 4, :], ps[:, 3 + g, :].rearrange("p (h n) -> p h n", h=4), ACT.Exp)
                    ins.then_inc(*S["seg_exp"].inc())

        @block.gpsimd
        def _(pool):
            pool.wait_ge(*S["a_ready"](1))
            for i in range(1, L2T):
                if i >= 3:
                    pool.wait_ge(*S["segments"](i - 2))
                for h in range(H):
                    ins = pool.tensor_scalar(aU[:, i % 2, h, :], c["gt"], sc[:, 1, i * H + h:i * H + h + 1], None, ALU.mult)
                ins.then_inc(*S["aU_ready"].inc())

        @block.vector
        def _(dve):
            step = chained(dve, S["dve"])
            flat = dt[:].rearrange("p t h -> p (t h)")
            dve.memset(xdt[:, H * HD:], 0.0)
            dve.memset(st[:], 0.0).then_inc(*S["state_zero"].inc())
            dve.tensor_tensor(dt[:], dt[:], spread(dtb, [P, L2T, H], 1), ALU.add).then_inc(*S["dt_biased"].inc())
            dve.wait_ge(*S["log1p"](1))
            step(dve.scalar_tensor_tensor(out=sc[:, 2, :], in0=flat, scalar=0.0, in1=sc[:, 0, :], op0=ALU.max, op1=ALU.add))
            step(dve.tensor_scalar(sc[:, 2, 0:H], sc[:, 2, 0:H], c["valid"], None, ALU.mult))
            dve.wait_ge(*S["a_exp"](1))
            step(dve.tensor_tensor(sc[:, 1, :].rearrange("p (t h) -> p t h", h=H), sc[:, 2, :].rearrange("p (t h) -> p t h", h=H),
                                   spread(par[:, 24:32], [P, L2T, H], 1), ALU.mult))
            dve.tensor_scalar(sc[:, 1, :], sc[:, 1, :], -1.0, None, ALU.mult).then_inc(*S["a_ready"].inc())
            dve.wait_ge(*S["decays"](1))
            for i in range(L2T):
                hs = slice(i * H, (i + 1) * H)
                x = heads(xt[:, i % 2, :])
                dve.wait_ge(*S["xB_kept"](i + 1))
                if i >= 2:
                    dve.wait_ge(*S["diag_done"](i - 1))
                step(dve.tensor_tensor(heads(xdt[:, 0:H * HD]), x, spread(sc[:, 2, hs], [P, H, HD], 2), ALU.mult))
                if i < L2T - 1:
                    if i >= 1:
                        dve.wait_ge(*S["state_sum"](i))
                    dve.tensor_tensor(heads(xend[:]), heads(xdt[:, 0:H * HD]), spread(E[:, 1, hs], [P, H, HD], 2), ALU.mult)\
                       .then_inc(*S["xend_ready"].inc())
                if i >= 1:
                    dve.wait_ge(*S["cb_done"](i))
                    step(dve.tensor_tensor(cbm[:], ps[:, 2, 0:2 * P].rearrange("p (g n) -> p g n", g=2),
                                           spread(c["le"], [P, 2, P], 1), ALU.mult))
                    dve.wait_ge(*S["seg_exp"](i))
                    for g in range(2):
                        ins = dve.tensor_tensor(W[:, 4 * g:4 * g + 4, :], W[:, 4 * g:4 * g + 4, :],
                                                spread(cbm[:, g, :], [P, 4, P], 1), ALU.mult)
                    ins.then_inc(*S["W_ready"].inc())
                if i < L2T - 1:
                    if i >= 1:
                        dve.wait_ge(*S["off_done"](i))
                    else:
                        dve.wait_ge(*S["state_zero"](1))
                    s3 = heads(st[:])
                    step(dve.tensor_tensor(s3, s3, spread(E[:, 2, hs], [P, H, HD], 2), ALU.mult))
                    dve.wait_ge(*S["state_sum"](i + 1))
                    dve.tensor_tensor(st[:], st[:], ps[:, 7, :], ALU.add).then_inc(*S["state_new"].inc())
                if i >= 1:
                    y = Y[:, i - 1, SBH * HD:SBH * HD + H * HD]
                    dve.wait_ge(*S["off_done"](i))
                    step(dve.tensor_tensor(heads(t1[:]), heads(ps[:, 5, :]), spread(E[:, 0, hs], [P, H, HD], 2), ALU.mult))
                    dve.wait_ge(*S["diag_done"](i))
                    for g, bank in enumerate((6, 1)):
                        tg = heads(t1[:])[:, 4 * g:4 * g + 4, :]
                        ins = dve.tensor_tensor(tg, tg, ps[:, bank, :].rearrange("p (h d) -> p h d", h=4)[:, :, 0:HD], ALU.add)
                    step(ins)
                    step(dve.tensor_tensor(heads(t2[:]), x, spread(dskip, [P, H, HD], 2), ALU.mult))
                    step(dve.tensor_tensor(t1[:], t1[:], t2[:], ALU.add))
                    dve.tensor_tensor(y, y, t1[:], ALU.mult).then_inc(*S["y_out"].inc())

        @block.tensor
        def _(pe):
            pe.wait_ge(*S["a_ready"](1))
            for n, m in enumerate(("le", "gt", "one")):
                mm = pe.matmul(ps[:, 0, n * NH:(n + 1) * NH], c[m], sc[:, 1, :], start=True, stop=True)
            mm.then_inc(*S["decay_sums"].inc())
            pe.wait_ge(*S["decays"](1))
            for i in range(L2T):
                ch = slice(i * P, (i + 1) * P)
                if i >= 1:
                    pe.wait_ge(*S["xB_kept"](i))
                for b in range(4):
                    pe.transpose(ps[:, 0, b * P:(b + 1) * P], convT[:, b, ch], c["ident"])
                if i >= 2:
                    pe.wait_ge(*S["y_out"](i - 1))
                for b in range(2):
                    mm = pe.transpose(ps[:, 1, b * P:(b + 1) * P], convT[:, 4 + b, ch], c["ident"])
                mm.then_inc(*S["turned"].inc())
                if i >= 1:
                    if i >= 2:
                        pe.wait_ge(*S["W_ready"](i - 1))
                    for g in range(2):
                        mm = pe.matmul(ps[:, 2, g * P:(g + 1) * P], convT[:, 4 + g, ch], convT[:, 6 + g, ch], start=True, stop=True)
                    mm.then_inc(*S["cb_done"].inc())
                    pe.wait_ge(*S["aU_ready"](i))
                    for h in range(H):
                        mm = pe.matmul(ps[:, 3 + h // 4, (h % 4) * P:(h % 4 + 1) * P], aU[:, i % 2, h, :], c["le"],
                                       start=True, stop=True)
                    mm.then_inc(*S["segments"].inc())
                    pe.wait_ge(*S["state_new"](i))
                    if i >= 2:
                        pe.wait_ge(*S["y_out"](i - 1))
                    for g in range(SSDG):
                        mm = pe.matmul(ps[:, 5, g * GW:(g + 1) * GW], convT[:, 6 + g, ch], st[:, g * GW:(g + 1) * GW],
                                       start=True, stop=True)
                    mm.then_inc(*S["off_done"].inc())
                if i < L2T - 1:
                    pe.wait_ge(*S["xend_ready"](i + 1))
                    if i >= 1:
                        pe.wait_ge(*S["state_new"](i))
                    for g in range(SSDG):
                        mm = pe.matmul(ps[:, 7, g * GW:(g + 1) * GW], Bt[:, i % 2, g * P:(g + 1) * P], xend[:, g * GW:(g + 1) * GW],
                                       start=True, stop=True)
                    mm.then_inc(*S["state_sum"].inc())
                if i >= 1:
                    pe.wait_ge(*S["W_ready"](i))
                    if i >= 2:
                        pe.wait_ge(*S["y_out"](i - 1))
                    for h in range(H):
                        at = (h % 4) * P
                        mm = pe.matmul(ps[:, (6, 1)[h // 4], at:at + WIDE], W[:, h, :], xdt[:, h * HD:h * HD + WIDE],
                                       start=True, stop=True)
                    mm.then_inc(*S["diag_done"].inc())
    pr.end()


def stage_hg_project(pr, hT, qk, Kt, LF, Vh, Y, c, work):
    nc, S, ps = pr.nc, pr.S, pr.ps
    i0 = pr.next_use
    n = L2T
    W = HGH * HD
    rot, sg = work["rot"], work["sg"]
    LOG_TINY = math.log(1e-30)
    LAG = 1
    with nc.Block() as block:
        @block.sync
        def _(sp):
            pr.load_more(sp, 2)

        @block.tensor
        def _(pe):
            def turn(t):
                pe.wait_ge(*S["k_ready"](t + 1))
                if t >= 1:
                    pe.wait_ge(*S["qkT_kept"](t))
                for b in range(4):
                    mm = pe.transpose(ps[:, 4, b * P:(b + 1) * P], rot[:, t % 2, b * P:(b + 1) * P], c["ident"])
                mm.then_inc(*S["qkT_ready"].inc())

            for u in range(2 * n):
                t = u % n
                if u % n == 0:
                    pr.arrived(pe, i0 + u // n)
                w = pr.view(i0 + u // n)
                if u >= 2:
                    pe.wait_ge(*(S["f_used"](u - 1) if u - 2 < n else S["v_used"](u - 1 - n)))
                for k in range(KC):
                    mm = pe.matmul(ps[:, u % 2, :], hT[:, k, t * P:(t + 1) * P], w[:, k, :], start=(k == 0), stop=(k == KC - 1))
                mm.then_inc(*S["proj_done"].inc())
                if t == n - 1:
                    pe.wait_ge(*S["proj_done"](u + 1))
                    pe.sem_inc(pr.spent, 1)
                if LAG <= u < n + LAG:
                    turn(u - LAG)

        @block.scalar
        def _(act):
            step = chained(act, S["act"])

            def keep(t):
                act.wait_ge(*S["qkT_ready"](t + 1))
                act.activation(qk[:, :, t * P:(t + 1) * P], ps[:, 4, :].rearrange("p (b n) -> p b n", b=4), ACT.Copy)\
                   .then_inc(*S["qkT_kept"].inc())

            for t in range(n):
                act.wait_ge(*S["proj_done"](t + 1))
                if t >= 2:
                    act.wait_ge(*S["qkT_ready"](t - 1))
                    act.wait_ge(*S["k_ready"](t - 1))
                act.activation(rot[:, t % 2, 0:W], ps[:, t % 2, 0:W], ACT.Silu)
                step(act.activation(sg[:, t % 2, 0, :], ps[:, t % 2, W:2 * W], ACT.Abs))
                step(act.activation(sg[:, t % 2, 0, :], sg[:, t % 2, 0, :], ACT.Exp, scale=-1.0))
                act.activation(sg[:, t % 2, 0, :], sg[:, t % 2, 0, :], ACT.Ln, bias=1.0).then_inc(*S["log1p"].inc())
                act.wait_ge(*S["f_used"](t + 1))
                act.activation(Kt[:, t, :], sg[:, t % 2, 2, :], ACT.Exp, scale=-1.0).then_inc(*S["k_exp"].inc())
                if t >= 1:
                    keep(t - 1)
            for t in range(n):
                act.wait_ge(*S["proj_done"](n + t + 1))
                b = (n + t) % 2
                ins = act.activation(Vh[:, t, 0:W], ps[:, b, 0:W], ACT.Copy)
                if t:
                    ins = act.activation(Y[:, t - 1, 3 * W:4 * W], ps[:, b, W:2 * W], ACT.Silu)
                ins.then_inc(*S["v_used"].inc())
                if t == 0:
                    keep(n - 1)

        @block.gpsimd
        def _(pool):
            pool.memset(Vh[:, :, W:], 0.0)

        @block.vector
        def _(dve):
            step = chained(dve, S["dve"])
            for t in range(n):
                f = ps[:, t % 2, W:2 * W]
                l1, a, b = (sg[:, t % 2, i, :] for i in range(3))
                dve.wait_ge(*S["log1p"](t + 1))
                if t >= 2:
                    dve.wait_ge(*S["k_exp"](t - 1))
                step(dve.tensor_scalar(a, f, -1.0, 0.0, ALU.mult, ALU.max))
                step(dve.scalar_tensor_tensor(out=b, in0=f, scalar=0.0, in1=l1, op0=ALU.max, op1=ALU.add))
                step(dve.tensor_tensor(a, a, l1, ALU.add))
                ins = dve.tensor_scalar(LF[:, t, :], a, -LOG_TINY, -1.0, ALU.min, ALU.mult)
                if t == 0:
                    step(ins)
                    ins = dve.tensor_scalar(LF[:, t, :], LF[:, t, :], c["valid"], None, ALU.mult)
                ins.then_inc(*S["f_used"].inc())
                dve.wait_ge(*S["k_exp"](t + 1))
                if t == 0:
                    step(dve.tensor_scalar(Kt[:, t, :], Kt[:, t, :], c["valid"], None, ALU.mult))
                dve.tensor_copy(rot[:, t % 2, W:2 * W], Kt[:, t, :]).then_inc(*S["k_ready"].inc())
    pr.end(2)


def stage_hg(pr, qk, Kt, LF, Vh, OH, c, b_):
    nc, S, ps = pr.nc, pr.S, pr.ps
    EX, Qt, Kl, Qg, EE, kend, Sm, st, dec = (b_[k] for k in ("EX", "Qt", "Kl", "Qg", "EE", "kend", "Sm", "state", "decay"))
    TW = 3 * P
    n = L2T
    with nc.Block() as block:
        @block.tensor
        def _(pe):
            def sums(i, fb):
                if 2 * i + fb >= 1:
                    pe.wait_ge(*S["decayed"](2 * i + fb))
                for q in range(3):
                    mm = pe.matmul(ps[:, q, 0:TW], LF[:, i, fb * P:(fb + 1) * P], c["levels"][:, q * TW:(q + 1) * TW],
                                   start=True, stop=True)
                mm.then_inc(*S["sums"].inc())

            def end_sums(i):
                if i >= 1:
                    pe.wait_ge(*S["state_new"](i))
                    pe.wait_ge(*S["decayed"](2 * i + 2))
                for fb in range(2):
                    mm = pe.matmul(ps[:, fb, TW:BANK], c["gt"], LF[:, i, fb * P:(fb + 1) * P], start=True, stop=True)
                mm.then_inc(*S["end_sums"].inc())

            def scores(i, h):
                fb, r, ch = h // 2, slice(64 * (h % 2), 64 * (h % 2) + 64), slice(i * P, (i + 1) * P)
                j = (i - 1) * HGH + h
                if j >= 2:
                    pe.wait_ge(*S["masked"](j - 1))
                for v in range(LEVELS + 1):
                    k_, q_ = (Kl[r, i % 2, fb, v, :], Qt[r, i % 2, fb, v, :]) if v < LEVELS else (qk[r, 2 + fb, ch], qk[r, fb, ch])
                    mm = pe.matmul(ps[:, 4 + 2 * (h % 2) + v // 4, (v % 4) * P:(v % 4 + 1) * P], k_, q_, start=True, stop=True)
                mm.then_inc(*S["scored"].inc())

            sums(0, 0)
            sums(0, 1)
            for i in range(n):
                if i >= 1:
                    pe.wait_ge(*S["q_levels"](i + 1))
                    pe.wait_ge(*S["k_levels"](i))
                    scores(i, 0)
                else:
                    pe.wait_ge(*S["decayed"](2))
                end_sums(i)
                if i >= 2:
                    pe.wait_ge(*S["o_kept"](i - 1))
                for h in range(HGH):
                    if i >= 1:
                        if h + 1 < HGH:
                            scores(i, h + 1)
                        fb, r = h // 2, slice(64 * (h % 2), 64 * (h % 2) + 64)
                        j = (i - 1) * HGH + h
                        pe.wait_ge(*S["masked"](j + 1))
                        o = ps[:, 3, h * P:h * P + HD]
                        for v in range(LEVELS + 1):
                            pe.matmul(ps[:, 3, h * P:h * P + WIDE], Sm[:, h % 2, v, :], Vh[:, i, h * HD:h * HD + WIDE],
                                      start=(v == 0), stop=(v == LEVELS), skip_group_check=True)
                        if j >= 1:
                            pe.wait_ge(*S["o_done"](j))
                        pe.matmul(o, Qg[r, i % 2, fb, :], st[r, fb, :], start=False, stop=True, skip_group_check=True)\
                          .then_inc(*S["o_done"].inc())
                    if h < 2 and i + 1 < n:
                        if h == 0:
                            pe.wait_ge(*S["end_decayed"](i + 1))
                        sums(i + 1, h)
                pe.wait_ge(*S["kend_ready"](i + 1))
                if i + 1 < n:
                    pe.wait_ge(*S["decayed"](2 * i + 4))
                for fb in range(2):
                    mm = pe.matmul(ps[:, fb, TW:BANK], kend[:, fb * P:(fb + 1) * P], Vh[:, i, fb * P:(fb + 1) * P],
                                   start=True, stop=True)
                mm.then_inc(*S["state_sum"].inc())

        @block.scalar
        def _(act):
            def decay(i, fb):
                act.wait_ge(*S["sums"](2 * i + fb + 1))
                if fb == 0 and i >= 1:
                    act.wait_ge(*S["q_levels"](i))
                    if i >= 2:
                        act.wait_ge(*S["k_levels"](i - 1))
                act.activation(EX[:, fb, :, :].rearrange("p v n -> p (v n)").rearrange("p (a n) -> p a n", a=3),
                               ps[:, 0:3, 0:TW], ACT.Exp).then_inc(*S["decayed"].inc())

            decay(0, 0)
            decay(0, 1)
            for i in range(n):
                act.wait_ge(*S["end_sums"](i + 1))
                if i >= 1:
                    act.wait_ge(*S["kend_ready"](i))
                act.activation(EE[:].rearrange("p (b n) -> p b n", b=2), ps[:, 0:2, TW:BANK], ACT.Exp)\
                   .then_inc(*S["end_decayed"].inc())
                if i + 1 < n:
                    decay(i + 1, 0)
                    decay(i + 1, 1)

        @block.gpsimd
        def _(pool):
            for i in range(n):
                if i >= 1:
                    pool.wait_ge(*S["state_sum"](i))
                pool.wait_ge(*S["end_decayed"](i + 1))
                pool.tensor_tensor(kend[:], EE[:], Kt[:, i, :], ALU.mult).then_inc(*S["kend_ready"].inc())
                if i + 1 < n:
                    nx, ch = i + 1, slice((i + 1) * P, (i + 2) * P)
                    if i >= 2:
                        pool.wait_ge(*S["scored"](HGH * (i - 1)))
                    for fb in range(2):
                        pool.wait_ge(*S["decayed"](2 * nx + fb + 1))
                        ins = pool.tensor_tensor(Kl[:, nx % 2, fb, :, :], EX[:, fb, 0:LEVELS, :],
                                                 spread(qk[:, 2 + fb, ch], [P, LEVELS, P], 1), ALU.mult)
                    ins.then_inc(*S["k_levels"].inc())

        @block.vector
        def _(dve):
            def q_levels(i, fb):
                ch = slice(i * P, (i + 1) * P)
                dve.wait_ge(*S["decayed"](2 * i + fb + 1))
                if i >= 1:
                    if i >= 3:
                        dve.wait_ge(*S["o_done"](HGH * (i - 2)))
                    dve.tensor_tensor(Qt[:, i % 2, fb, :, :], EX[:, fb, 0:LEVELS, :], spread(qk[:, fb, ch], [P, LEVELS, P], 1),
                                      ALU.mult)
                    dve.tensor_tensor(Qg[:, i % 2, fb, :], EX[:, fb, LEVELS, :], qk[:, fb, ch], ALU.mult)
                ins = dve.tensor_copy(dec[:, i % 2, fb:fb + 1], EX[:, fb, LEVELS, P - 1:P])
                if fb == 1:
                    ins.then_inc(*S["q_levels"].inc())

            dve.memset(st[:], 0.0).then_inc(*S["state_zero"].inc())
            dve.wait_ge(*S["state_zero"](1))
            q_levels(0, 0)
            q_levels(0, 1)
            for i in range(n):
                for h in range(HGH):
                    if i >= 1:
                        j = (i - 1) * HGH + h
                        dve.wait_ge(*S["scored"](j + 1))
                        if j >= 2:
                            dve.wait_ge(*S["o_done"](j - 1))
                        dve.tensor_tensor(Sm[:, h % 2, :, :].rearrange("p v n -> p (v n)").rearrange("p (a n) -> p a n", a=2),
                                          ps[:, 4 + 2 * (h % 2):6 + 2 * (h % 2), :],
                                          c["pairs"].rearrange("p (a n) -> p a n", a=2), ALU.mult).then_inc(*S["masked"].inc())
                    if h % 2 == 1 and i + 1 < n:
                        q_levels(i + 1, h // 2)
                if i >= 1:
                    dve.wait_ge(*S["o_done"](HGH * i))
                    dve.tensor_copy(OH[:, i - 1, :].rearrange("p (h d) -> p h d", h=HGH),
                                    ps[:, 3, :].rearrange("p (h d) -> p h d", h=HGH)[:, :, 0:HD]).then_inc(*S["o_kept"].inc())
                dve.wait_ge(*S["q_levels"](i + 1))
                dve.wait_ge(*S["state_sum"](i + 1))
                for fb in range(2):
                    for half in range(2):
                        r = slice(64 * half, 64 * half + 64)
                        ins = dve.scalar_tensor_tensor(out=st[r, fb, :], in0=st[r, fb, :], scalar=dec[r, i % 2, fb:fb + 1],
                                                       in1=ps[r, fb, TW + 64 * half:TW + 64 * half + 64],
                                                       op0=ALU.mult, op1=ALU.add)
                ins.then_inc(*S["state_new"].inc())
                dve.wait_ge(*S["state_new"](i + 1))
    pr.end()


INPUTS = {"x": (SEQ, D), "ctx": (CTX, D), "cols": (P, 2 * KC), "w_ada": (LAYERS, D, 3 * D), "w_in": (LAYERS, D, 3584),
          "w_out": (LAYERS, D, D), "small": (LAYERS, P, 600), "bgate": (LAYERS, P, D), "rpb": (LAYERS, RPB_N),
          "meta": (16, D), "w_in2": (D, 3336), "w_out2": (D, D), "w_up": (D, FF), "w_down": (FF, D), "small2": (P, 1232),
          "const1": (P, N1), "const2": (P, N2)}


def by_k(w):
    return w.rearrange("(k p) n -> p k n", p=P)


def plan_weights(io):
    chunks = []

    def add(w, *pieces):
        chunks.append(([by_k(w)[:, :, a:b] for a, b in pieces], KC, sum(b - a for a, b in pieces)))

    for l in range(LAYERS):
        for n in range(6):
            add(io["w_ada"][l], (n * BANK, (n + 1) * BANK))
        for a, b in ((A_Q, A_V), (A_V, B_Q), (B_Q, B_V), (B_V, C_Q), (C_Q, C_K), (C_K, C_V), (C_V, C_G), (C_G, 3584)):
            add(io["w_in"][l], (a, b))
        for h in range(2):
            add(io["w_out"][l], (h * BANK, (h + 1) * BANK))
    w = io["w_in2"]
    add(w, (S_Q, S_V))
    add(w, (S_V, S_Z1))
    add(w, (S_Z1, S_X), (S_DT, H_Q))
    add(w, (S_X, S_B))
    add(w, (S_B, S_DT))
    add(w, (H_Q, H_I))
    add(w, (H_I, 3336))
    for h in range(2):
        add(io["w_out2"], (h * BANK, (h + 1) * BANK))
    for half in range(2):
        for n in range(FF // BANK):
            add(io["w_up"], (n * BANK, (n + 1) * BANK))
        for n in range(FF // BANK):
            chunks.append(([by_k(io["w_down"][n * BANK:(n + 1) * BANK, :])], 4, D))
    return chunks


def banks_of(ranges):
    banks, blocks, col = [[]], [], 0
    for start, width, biased in ranges:
        done = 0
        while done < width:
            used = sum(p["w"] for p in banks[-1])
            if used == BANK:
                banks.append([])
                used = 0
            w = min(width - done, BANK - used)
            banks[-1].append({"at": used, "w": w, "key": start + done, "col": col, "bias": biased, "off": done})
            blocks += [(col + b, start + done + b) for b in range(0, w, P)]
            done += w
            col += w
    return banks, blocks


def unit(qt, ranges, **more):
    banks, blocks = banks_of(ranges)
    return {"qt": qt, "banks": banks, "blocks": blocks, **more}


def layer(pr, l, io, T, const, x_src, ctx_src, dst):
    nc = pr.nc
    hT, Y, gate, small, sc, sh = (T[k] for k in ("hT", "Y", "gate", "small", "sc", "sh"))
    last = l == LAYERS - 1
    queries = range(XT) if last else range(NT)
    ident = const["ident"]
    gains = small[:, 152:600].rearrange("p (g d) -> p g d", d=HD)
    with ExitStack() as s:
        sb = lambda name, shape: s.enter_context(nc.sbuf_tensor(f"{name}_{l}", shape, F32))
        csilu, crep, bgate = sb("csilu", [P, 2 * KC]), sb("crep", [P, 2, KC, P]), sb("bgate", [P, D])
        stage_ada(pr, l, {
            "c": T["cols"], "csilu": csilu, "crep": crep, "bgate": bgate, "ident": ident, "gate": gate, "sc": sc, "sh": sh,
            "ng": small[:, 0:8], "bada": small[:, 8:24], "lamv": small[:, 24:152].rearrange("p (m d) -> p m d", d=DIFF_D),
            "gains": gains, "lam": T["lam"], "lamj": T["lamj"],
            "layer_loads": lambda l: [(small[:], io["small"][l]), (bgate[:], io["bgate"][l])]})
    whole = slice(0, P)
    with nc.sbuf_tensor(f"junk_{l}", [P, D + 16], F32) as junk:
        pr.junk = junk
        rows = [[(whole, x_src(t))] for t in range(XT)] + [[(whole, ctx_src(t))] for t in range(CT)]
        stage_norm(pr, rows, Y, T["ssq"], T["rs"], hT, lambda t, k: sc[:, k, t // XT:t // XT + 1],
                   lambda t, k: sh[:, k, t // XT:t // XT + 1], ident, ())

    every = list(range(NT))
    rope_a = (const["cosA"].rearrange("p (t d) -> p t d", d=DIFF_D), const["sinA"].rearrange("p (t d) -> p t d", d=DIFF_D))
    rope_b = (const["cosB"].rearrange("p (t d) -> p t d", d=HD), const["sinB"].rearrange("p (t d) -> p t d", d=HD))

    def group(name, blocks, vheads, chunks):
        s = ExitStack()
        qk = s.enter_context(nc.sbuf_tensor(f"qk_{name}_{l}", [P, blocks, NT * P], F32))
        Vw = s.enter_context(nc.sbuf_tensor(f"v_{name}_{l}", [P, NT, vheads * (HD + 1) + WIDE - HD - 1], F32))
        V = Vw[:, :, 0:vheads * (HD + 1)].rearrange("p t (h d) -> p t h d", d=HD + 1)
        with ExitStack() as w:
            sb = lambda nm, shape: w.enter_context(nc.sbuf_tensor(f"{nm}_{name}_{l}", shape, F32))
            work = {"sq": sb("sq", [P, 2, BANK]), "nrm": sb("nrm", [P, 2, BANK]), "rot": sb("rot", [P, 2, BANK]),
                    "tmp": sb("tmp", [P, BANK]), "st": sb("st", [P, 2, 3, 16]), "ident": ident,
                    "ones_of": (V[:, :, :, HD:HD + 1], Vw[:, :, vheads * (HD + 1):])}
            stage_project(pr, hT, chunks(qk, V), work)
        return s, qk, Vw

    def headed(dst, b0, dim, n_heads, gain, rope=None, tiles=every):
        return {"heads": True, "parts": [], "dst": dst, "b0": b0, "dim": dim, "n_heads": n_heads, "gain": gain, "rope": rope,
                "width_heads": dim * n_heads, "tiles": list(tiles)}

    def parts(*p, tiles=every):
        return {"heads": False, "parts": list(p), "tiles": list(tiles)}

    def gate_to(a, b):
        return lambda t: Y[:, t, a:b] if t in queries else None

    def attend(name, qk, V, units, post, pmax, smax=None, bias=None, prepare=None):
        with ExitStack() as w:
            sb = lambda nm, shape: w.enter_context(nc.sbuf_tensor(f"{nm}_{name}_{l}", shape, F32))
            Pb, PT, small_ = sb("P", [P, 2, pmax]), sb("PT", [P, 2, pmax // P, P]), sb("max", [P, 2, 16])
            Ssb = sb("S", [P, 2, smax]) if smax else None
            stage_attend(pr, units, qk, V, Pb, Ssb, PT, small_, ident, post, bias=bias, prepare=prepare)

    def keys(t):
        return [(0, NT * P, False)] if t < XT else [(XT * P, CTX, False)]

    rinv = T["rinv"]

    def post_plain(col0):
        def post(dve, step, u, o, i):
            r = rinv[:, 0:1]
            step(dve.reciprocal(r, o[:, HD:HD + 1]))
            y = Y[:, u["qt"], col0 + u["h"] * HD:col0 + (u["h"] + 1) * HD]
            return dve.scalar_tensor_tensor(out=y, in0=o[:, 0:HD], scalar=r, in1=y, op0=ALU.mult, op1=ALU.mult)
        return post

    s, qk, V = group("a", 4, AH, lambda qk, V: [
        headed(qk, 0, DIFF_D, 16, [(gains[:, 0, 0:DIFF_D], 0, 8, plain), (gains[:, 1, 0:DIFF_D], 8, 16, plain)], rope_a),
        parts(("copy", 0, 256, lambda t: V[:, t, :, 0:HD]), ("silu", 256, 512, gate_to(0, 256)))])
    with s:
        with nc.sbuf_tensor(f"oa_{l}", [P, NT, AH * HD], F32) as OA:
            lam = T["lam"]

            def post_a(dve, step, u, o, i):
                r, mine = rinv[:, 0:1], OA[:, u["qt"], u["h"] * HD:(u["h"] + 1) * HD]
                step(dve.reciprocal(r, o[:, HD:HD + 1]))
                if u["map"] == 0:
                    return dve.tensor_scalar(mine, o[:, 0:HD], r, None, ALU.mult)
                step(dve.tensor_scalar(r, r, lam[:, 5:6], None, ALU.mult))
                return dve.scalar_tensor_tensor(out=mine, in0=o[:, 0:HD], scalar=r, in1=mine, op0=ALU.mult, op1=ALU.add)

            units = [unit(t, keys(t), h=h, vh=h, map=m, rows=slice(32 * ((2 * h + m) % 4), 32 * ((2 * h + m) % 4) + 32),
                          qb=(2 * h + m) // 4, kb=2 + (2 * h + m) // 4)
                     for h in range(AH) for t in queries for m in range(2)]
            attend("a", qk, V, units, post_a, NT * P)
            with nc.sbuf_tensor(f"sqn_{l}", [P, 2, 256], F32) as sq, nc.sbuf_tensor(f"stn_{l}", [P, 3, 40], F32) as st:
                stage_head_norm(pr, lambda t: OA[:, t, :], len(queries), AH, gains[:, 6, :], st, lambda t: Y[:, t, 0:256], sq, False)

    s, qk, V = group("b", 4, BKV, lambda qk, V: [
        headed(qk, 0, HD, 8, [(gains[:, 2, :], 0, BH, kv_halves), (gains[:, 3, :], BH, 8, plain)], rope_b),
        parts(("copy", 0, 128, lambda t: V[:, t, :, 0:HD]), ("silu", 128, 512, gate_to(256, 640)))])
    with s:
        units = [unit(t, keys(t), h=h, vh=h // 3, rows=slice(64 * (h // 3), 64 * (h // 3) + 64), qb=h % 3, kb=3)
                 for h in range(BH) for t in queries]
        attend("b", qk, V, units, post_plain(256), NT * P)

    s, qk, V = group("c", 6, CH, lambda qk, V: [
        headed(qk, 0, HD, CH, [(gains[:, 4, :], 0, CH, plain)], tiles=queries),
        headed(qk, 3, HD, CH, [(gains[:, 5, :], 0, CH, plain)]),
        parts(("copy", 0, 384, lambda t: V[:, t, :, 0:HD])),
        parts(("silu", 0, 384, gate_to(640, 1024)), tiles=queries)])
    flat = hT[:].rearrange("p k n -> p (k n)")
    TF = flat[:, 0:CH * JT * GRID].rearrange("p (h n) -> p h n", h=CH)
    TI = flat[:, CH * JT * GRID:CH * (JT + JI) * GRID].rearrange("p (h n) -> p h n", h=CH)
    S = pr.S

    def rows4(ap, j):
        return ap.rearrange("p h (j c) -> p h j c", j=j)

    def load_bias(sp):
        sp.wait_ge(pr.bias_shifted, 16 * LAYERS * CH)
        for half in range(2):
            sp.dma_start(rows4(TF, JT)[64 * half:64 * half + 64], io["rpb_shifted"][l, :, :, 1 - half:1 - half + JT, :])\
              .then_inc(*S["bias_in"].inc(16))

    def mask_bias(dve, step):
        dve.wait_ge(*S["bias_in"](16 * 2))
        t3 = flat[:, 0:CH * JT * GRID].rearrange("p (j c) -> p j c", c=GRID)
        step(dve.tensor_tensor(t3, t3, spread(const["in"], [P, CH * JT, GRID], 1), ALU.mult))
        step(dve.tensor_tensor(t3, t3, spread(const["neg"], [P, CH * JT, GRID], 1), ALU.add))
        step(dve.tensor_copy(rows4(TI, JI), rows4(TF, JT)[:, :, 2:2 + JI, :]))
        step(dve.memset(rows4(TI, JI)[0:64, :, 8:10, :], NEG))
        step(dve.memset(rows4(TI, JI)[64:128, :, 0:1, :], NEG))
        step(dve.memset(rows4(TI, JI)[64:128, :, 9:10, :], NEG))

    def bias(u, piece):
        t = u["qt"]
        if 2 <= t <= 5:
            return TI[:, u["h"], piece["off"]:piece["off"] + piece["w"]]
        slot = (0 if t < 2 else 8) - 2 * t + 6
        return TF[:, u["h"], slot * GRID + piece["off"]:slot * GRID + piece["off"] + piece["w"]]

    def window(t):
        if t >= XT:
            return [(XT * P, CTX, False)]
        first, tiles = (0, 4) if t < 2 else (4, 4) if t > 5 else (t - 2, 5)
        return [(first * P, tiles * P, True), (XT * P, CTX, False)]

    with s:
        units = [unit(t, window(t), h=h, vh=h, rows=slice(64 * (h % 2), 64 * (h % 2) + 64), qb=h // 2, kb=3 + h // 2)
                 for h in range(CH) for t in queries]
        attend("c", qk, V, units, post_plain(640), 7 * P, smax=5 * P, bias=bias,
               prepare={"sync": load_bias, "gpsimd": lambda pool: None, "vector": mask_bias})

    with ExitStack() as w:
        sb = lambda nm, shape: w.enter_context(nc.sbuf_tensor(f"{nm}_{l}", shape, F32))
        stage_out(pr, list(queries), Y, sb("yT", [P, 2, KC, P]), lambda t: x_src(t) if t < XT else ctx_src(t - XT),
                  dst, lambda t: gate[:, t // XT, :], sb("xt", [P, 2, D]), sb("res", [P, 2, D]), ident)


def build(nc, io, out):
    pr = Program(nc, io)
    pr.chunks = plan_weights(io)
    io["rpb_pad"] = nc.dram_tensor("rpb_pad", (LAYERS, RPB_N + 2 * SLACK), F32, kind="Internal").ap()
    io["rpb_shifted"] = nc.dram_tensor("rpb_shifted", (LAYERS, GRID, CH, RPB_R, GRID), F32, kind="Internal").ap()
    x1 = nc.dram_tensor("x1", (NT * P, D), F32, kind="Internal").ap()
    x2 = nc.dram_tensor("x2", (SEQ, D), F32, kind="Internal").ap()
    x3 = nc.dram_tensor("x3", (SEQ, D), F32, kind="Internal").ap()

    def rows(ap):
        return lambda t: ap[t * P:(t + 1) * P, :]

    with ExitStack() as s:
        sb = lambda name, *shape: s.enter_context(nc.sbuf_tensor(name, list(shape), F32))
        c1 = sb("const1", P, N1)
        T = {"hT": sb("hT", P, KC, NT * P), "Y": sb("Y", P, NT, D), "gate": sb("gate", P, 2, D), "small": sb("small", P, 600),
             "sc": sb("sc", P, KC, 2), "sh": sb("sh", P, KC, 2), "lam": sb("lam", P, 8), "lamj": sb("lamj", P, 2, DIFF_D),
             "ssq": sb("ssq", P, 16), "rs": sb("rs", P, 16), "rinv": sb("rinv", P, 2), "cols": sb("cols", P, 2 * KC)}
        const = {k: c1[:, a:b] for k, (a, b) in P1.items()}
        with nc.sbuf_tensor("zero", [1, SLACK], F32) as zero:
            stage_setup(pr, c1, io["const1"], [(T["cols"][:], io["cols"])], rpb=(io["rpb"], io["rpb_pad"], zero, io["rpb_shifted"]))
        layer(pr, 0, io, T, const, rows(io["x"]), rows(io["ctx"]), rows(x1))
        layer(pr, 1, io, T, const, rows(x1), lambda t: x1[(XT + t) * P:(XT + t + 1) * P, :], rows(x2))

    with ExitStack() as s:
        sb = lambda name, *shape: s.enter_context(nc.sbuf_tensor(name, list(shape), F32))
        c2, small = sb("const2", P, N2), sb("small2", P, 1240)
        ssq, rs = sb("ssq2", P, 16), sb("rs2", P, 16)
        c = {k: c2[:, a:b] for k, (a, b) in P2.items()}
        stage_setup(pr, c2, io["const2"], [(small[:, 0:1232], io["small2"])])
        whole = slice(0, P)
        with ExitStack() as m:
            sm = lambda name, *shape: m.enter_context(nc.sbuf_tensor(name, list(shape), F32))
            hT, Y, dt = sm("hT2", P, KC, L2T * P), sm("Y2", P, XT, D), sm("dt", P, L2T, SSDH)
            with nc.sbuf_tensor("h2", [P, L2T, D], F32) as big, nc.sbuf_tensor("junk2", [P, D + 16], F32) as junk:
                pr.junk = junk
                src = [[(slice(P - 16, P), io["meta"])]] + [[(whole, rows(x2)(t))] for t in range(XT)]
                stage_norm(pr, src, big, ssq, rs, hT, lambda t, k: small[:, k:k + 1], lambda t, k: 0.0, c["ident"], (0,))
            gq, gk = small[:, 16:80], small[:, 80:144]
            wide = {"sb": small[:, 144:400], "ssd": small[:, 400:912], "hg": small[:, 912:1168]}
            every = list(range(L2T))
            with nc.sbuf_tensor("qk_sb", [P, 4, L2T * P], F32) as qk, nc.sbuf_tensor("v_sb", [P, L2T, SBH * HD + WIDE - HD], F32) as V:
                with ExitStack() as w:
                    sw = lambda nm, shape: w.enter_context(nc.sbuf_tensor(f"{nm}_sb", shape, F32))
                    work = {"sq": sw("sq", [P, 2, BANK]), "nrm": sw("nrm", [P, 2, BANK]), "rot": sw("rot", [P, 2, BANK]),
                            "tmp": sw("tmp", [P, BANK]), "st": sw("st", [P, 2, 3, 16]), "ident": c["ident"],
                            "scale_of": (gq, HD ** -0.5), "ones_of": (V[:, :, SBH * HD:],)}
                    stage_project(pr, hT, [
                        {"heads": True, "parts": [], "dst": qk, "b0": 0, "dim": HD, "n_heads": 8, "width_heads": BANK,
                         "gain": [(gq, 0, 4, plain), (gk, 4, 8, plain)], "rope": None, "tiles": every},
                        {"heads": False, "tiles": every, "parts": [
                            ("copy", 0, 256, lambda t: V[:, t, 0:256]), ("silu", 256, 512, lambda t: Y[:, t - 1, 256:512] if t else None)]},
                        {"heads": False, "tiles": every, "parts": [
                            ("copy", 256, 264, lambda t: dt[:, t, :]), ("silu", 0, 256, lambda t: Y[:, t - 1, 512:768] if t else None)]},
                    ], work)
                with ExitStack() as w:
                    sw = lambda nm, *shape: w.enter_context(nc.sbuf_tensor(f"{nm}_st", list(shape), F32))
                    stage_stick(pr, qk, V, Y, c, {k: sw(k, P, 2, BANK) for k in ("mag", "sp", "sn", "w")} | {"acc": sw("acc", P, BANK)})
            def normed(name, lo, hi, heads, dim, o=None):
                with nc.sbuf_tensor(f"sqn_{name}", [P, 2, hi - lo], F32) as sq, nc.sbuf_tensor(f"stn_{name}", [P, 3, 40], F32) as st:
                    y = lambda t: Y[:, t, lo:hi]
                    stage_head_norm(pr, o or y, XT, heads, wide[name], st, y if o else None, sq, True, dim)

            normed("sb", 0, 256, SBH, HD)
            with nc.sbuf_tensor("convT", [P, 8, L2T * P], F32) as convT:
                with nc.sbuf_tensor("raw", [P, 2, 3 + L2T * P], F32) as raw:
                    stage_conv(pr, hT, convT, raw, small[:, 1168:1200].rearrange("p (b j) -> p b j", j=4), small[:, 1200:1208])
                with ExitStack() as w:
                    sw = lambda nm, *shape: w.enter_context(nc.sbuf_tensor(f"{nm}_ssd", list(shape), F32))
                    NH = L2T * SSDH
                    stage_ssd(pr, convT, Y, dt, small[:, 1208:1240], c, {
                        "aU": sw("aU", P, 2, SSDH, P), "xt": sw("xt", P, 2, BANK), "Bt": sw("Bt", P, 2, 2 * P),
                        "W": sw("W", P, SSDH, P), "xdt": sw("xdt", P, BANK + WIDE - HD), "xend": sw("xend", P, BANK), "state": sw("state", P, BANK),
                        "cbm": sw("cbm", P, 2, P), "E": sw("E", P, 3, NH), "t1": sw("t1", P, BANK), "t2": sw("t2", P, BANK),
                        "sc": sw("sc", P, 3, NH)})
            normed("ssd", 256, 768, SSDG, 256)
            with ExitStack() as w:
                sw = lambda nm, *shape: w.enter_context(nc.sbuf_tensor(f"{nm}_hg", list(shape), F32))
                qk, Kt, LF, Vh = sw("qk", P, 4, L2T * P), sw("K", P, L2T, 256), sw("LF", P, L2T, 256), sw("V", P, L2T, 256 + WIDE - HD)
                with nc.sbuf_tensor("rot_hg", [P, 2, BANK], F32) as rot, nc.sbuf_tensor("sg_hg", [P, 2, 3, 256], F32) as sg:
                    stage_hg_project(pr, hT, qk, Kt, LF, Vh, Y, c, {"rot": rot, "sg": sg})
                OH = sw("O", P, XT, 256)
                room = hT[:].rearrange("p k n -> p (k n)")[:, 0:8 * LEVELS * P].rearrange("p (a f v n) -> p a f v n", a=4, f=2, v=LEVELS)
                with ExitStack() as v:
                    sv = lambda nm, *shape: v.enter_context(nc.sbuf_tensor(f"{nm}_hgc", list(shape), F32))
                    stage_hg(pr, qk, Kt, LF, Vh, OH, c, {
                        "EX": sv("EX", P, 2, LEVELS + 2, P), "Qt": room[:, 0:2], "Kl": room[:, 2:4],
                        "Qg": sv("Qg", P, 2, 2, P), "decay": sv("decay", P, 2, 2), "EE": sv("EE", P, 256), "kend": sv("kend", P, 256),
                        "Sm": sv("Sm", P, 2, LEVELS + 1, P), "state": sv("state", P, 2, HD)})
                normed("hg", 768, 1024, HGH, HD, o=lambda t: OH[:, t, :])
            with ExitStack() as w:
                sw = lambda nm, *shape: w.enter_context(nc.sbuf_tensor(f"{nm}_o2", list(shape), F32))
                stage_out(pr, list(range(XT)), Y, sw("yT", P, 2, KC, P), rows(x2), rows(x3), lambda t: None, sw("xt", P, 2, D),
                          sw("res", P, 2, D), c["ident"])
        h2T = sb("h2T", P, KC, SEQ)
        with nc.sbuf_tensor("h3", [P, XT, D], F32) as big, nc.sbuf_tensor("junk3", [P, D + 16], F32) as junk:
            pr.junk = junk
            stage_norm(pr, [[(whole, rows(x3)(t))] for t in range(XT)], big, ssq, rs, h2T, lambda t, k: small[:, 8 + k:9 + k],
                       lambda t, k: 0.0, c["ident"], ())
        hid, xt, res = sb("hid", P, FF // P, BANK), sb("xt3", P, 2, D), sb("res3", P, 2, D)
        for half in range(2):
            at = lambda ap: (lambda t: ap[(4 * half + t) * P:(4 * half + t + 1) * P, :])
            stage_mlp_half(pr, h2T, hid, half * BANK, at(x3), at(out), xt, res, pr.out_stored, 64 * half)


def kernel(**inputs):
    import numpy as _np
    import concourse.bacc as _bacc
    from concourse import mybir as _mybir
    from concourse.bass_utils import run_bass_kernel_spmd as _run

    a = {k: _np.asarray(v) for k, v in inputs.items()}
    tall = lambda v: _np.broadcast_to(v.reshape(1, -1), (P, v.size))
    cols = lambda v: v.reshape(-1, P).T
    wide = lambda v: _np.concatenate([v, _np.zeros(HD - v.size, v.dtype)])
    small = [_np.concatenate([cols(a["norm_g"][l]), cols(a["b_ada"][l][:2 * D])]
                             + [tall(a[n][l]) for n in ("lambda_q1", "lambda_k1", "lambda_q2", "lambda_k2")]
                             + [tall(wide(a[n][l])) for n in ("diff_q_norm", "diff_k_norm", "gqa_q_norm", "gqa_k_norm",
                                                              "nat_q_norm", "nat_k_norm", "diff_subln")], axis=1)
             for l in range(LAYERS)]
    conv = a["ssd_conv_w_2"][0].T.reshape(8, P, 4).transpose(1, 0, 2).reshape(P, 32)
    small2 = _np.concatenate([cols(a["norm_mix_w_2"][0]), cols(a["norm_mlp_w_2"][0])]
                             + [tall(a[n][0]) for n in ("sb_q_norm_2", "sb_k_norm_2", "sb_out_norm_2", "ssd_norm_w_2",
                                                        "hg_out_norm_2")]
                             + [conv, cols(a["ssd_conv_b_2"][0])]
                             + [tall(a[n][0]) for n in ("ssd_dt_bias_2", "ssd_A_log_2", "ssd_D_2")], axis=1)
    const1, const2 = constants()
    laid = {
        "x": a["x"][0], "ctx": a["ctx"][0],
        "cols": _np.stack([a["c"][0], a["c_ctx"]]).reshape(2, KC, P).transpose(2, 1, 0).reshape(P, 2 * KC),
        "w_ada": a["w_ada"], "w_in": a["w_in"], "w_out": a["w_out"], "small": _np.stack(small),
        "bgate": _np.stack([tall(a["b_ada"][l][2 * D:]) for l in range(LAYERS)]), "rpb": a["nat_rpb"].reshape(LAYERS, RPB_N),
        "meta": a["meta_tokens_2"], "w_in2": a["w_in_2"][0], "w_out2": a["w_out_2"][0], "w_up": a["w_up_2"][0],
        "w_down": a["w_down_2"][0], "small2": small2, "const1": const1, "const2": const2,
    }
    nc = _bacc.Bacc("TRN2", target_bir_lowering=False, num_devices=1)
    arrays, io = {}, {}
    for name, v in laid.items():
        v = _np.ascontiguousarray(v)
        assert v.shape == INPUTS[name], (name, v.shape)
        arrays[f"in_{name}"] = v
        io[name] = nc.dram_tensor(f"in_{name}", v.shape, _mybir.dt.from_np(v.dtype), kind="ExternalInput").ap()
    out = nc.dram_tensor("out_dram", (SEQ, D), F32, kind="ExternalOutput").ap()
    build(nc, io, out)
    r = _run(nc, [arrays], core_ids=[0])
    return r.results[0]["out_dram"].reshape(1, SEQ, D)
```
